# Optimizing a Trainium2 kernel written in Bass

```python
import jax, jax.numpy as jnp
from jax import lax
import numpy as np

D_MODEL = 1024
BATCH = 1
SEQ = 512
DEPTH = 2

GRID_W = 64
CTX_LEN = 256
MIX_WIDTH = D_MODEL
RET_WIDTH = MIX_WIDTH // 2
RET_HEADS = 8
RET_HEAD_DIM = RET_WIDTH // RET_HEADS
FOURIER_WIDTH = MIX_WIDTH // 4
FOURIER_GROUPS = 4
CONV_WIDTH = MIX_WIDTH // 4
CONV_GROUPS = 4
CHUNK = 128
ROPE_BASE = 10000.0
FFN_HIDDEN = ((8 * D_MODEL // 3 + 127) // 128) * 128
EPS = 1e-6

Q0 = 0
K0 = Q0 + RET_WIDTH
V0 = K0 + RET_WIDTH
G0 = V0 + RET_WIDTH
F0 = G0 + RET_WIDTH
CB0 = F0 + FOURIER_WIDTH
CC0 = CB0 + CONV_WIDTH
CH0 = CC0 + CONV_WIDTH
IN_WIDTH = CH0 + CONV_WIDTH

kernel_name = 'hybrid_retention_fourier_shortconv_dit'

def rmsnorm(x, g=None):
    xf = x.astype(jnp.float32)
    y = xf * lax.rsqrt(jnp.mean(xf * xf, axis=-1, keepdims=True) + EPS)
    if g is not None:
        y = y * g.astype(jnp.float32)
    return y.astype(x.dtype)

def dwconv3(x, w):
    xp = jnp.pad(x, ((0, 0), (1, 1), (0, 0)))
    return xp[:, :-2] * w[0] + xp[:, 1:-1] * w[1] + xp[:, 2:] * w[2]

def axial_rope(T):
    rows = T // GRID_W
    row = jnp.repeat(jnp.arange(rows, dtype=jnp.float32), GRID_W)
    col = jnp.tile(jnp.arange(GRID_W, dtype=jnp.float32), rows)
    n_freq = RET_HEAD_DIM // 4
    freq = ROPE_BASE ** (-jnp.arange(n_freq, dtype=jnp.float32) / n_freq)
    ang = jnp.concatenate([row[:, None] * freq, col[:, None] * freq], axis=-1)
    return jnp.cos(ang)[None, :, None, :], jnp.sin(ang)[None, :, None, :]

def apply_rope(t, cos, sin):
    half = t.shape[-1] // 2
    t1, t2 = t[..., :half], t[..., half:]
    return jnp.concatenate([t1 * cos - t2 * sin, t1 * sin + t2 * cos], axis=-1)

def _to_chunks(t):
    B, T, H, d = t.shape
    return t.reshape(B, T // CHUNK, CHUNK, H, d)

def _state_decay(log_decay):
    i = jnp.arange(CHUNK, dtype=jnp.float32)
    zeta = jnp.exp(log_decay[:, None] * (CHUNK - 1.0 - i))
    return zeta, jnp.exp(log_decay * CHUNK)

def _chunk_states(kc, vc, log_decay, init):
    zeta, chunk_decay = _state_decay(log_decay)
    u = jnp.einsum('bnjhd,hj,bnjhe->nbhde', kc, zeta, vc)

    def step(state, u_n):
        return chunk_decay[None, :, None, None] * state + u_n, state

    final, prev = lax.scan(step, init, u)
    return prev, final

def retention_scan(q, k, v, log_decay, init):
    B, T, H, d = q.shape
    i = jnp.arange(CHUNK, dtype=jnp.float32)
    diff = i[:, None] - i[None, :]
    intra = jnp.where(diff >= 0, jnp.exp(log_decay[:, None, None] * jnp.maximum(diff, 0.0)), 0.0)
    xi = jnp.exp(log_decay[:, None] * (i + 1.0))
    qc, kc, vc = _to_chunks(q), _to_chunks(k), _to_chunks(v)
    scores = jnp.einsum('bnihd,bnjhd->bnhij', qc, kc) * intra
    o_intra = jnp.einsum('bnhij,bnjhe->bnihe', scores, vc)
    prev, final = _chunk_states(kc, vc, log_decay, init)
    o_cross = jnp.einsum('bnihd,hi,nbhde->bnihe', qc, xi, prev)
    return (o_intra + o_cross).reshape(B, T, H, d), final

def fourier_mix(f):
    B, T, Cf = f.shape
    fg = f.astype(jnp.float32).reshape(B, T, FOURIER_GROUPS, Cf // FOURIER_GROUPS)
    out = jnp.fft.fft2(fg, axes=(1, 3), norm='ortho').real
    return out.reshape(B, T, Cf).astype(f.dtype)

def _heads(a, B, T):
    return a.astype(jnp.float32).reshape(B, T, RET_HEADS, RET_HEAD_DIM)

def token_mixers(p, log_decay_f, log_decay_b, init_f, init_b, conv_w, rope):
    B, T, _ = p.shape
    q = _heads(p[..., Q0:K0], B, T)
    k = _heads(p[..., K0:V0], B, T) * RET_HEAD_DIM ** -0.5
    v = _heads(p[..., V0:G0], B, T)
    if rope is not None:
        cos, sin = rope
        q = apply_rope(q, cos, sin)
        k = apply_rope(k, cos, sin)
    o_f, s_f = retention_scan(q, k, v, log_decay_f, init_f)
    o_b, s_b = retention_scan(q[:, ::-1], k[:, ::-1], v[:, ::-1], log_decay_b, init_b)
    o = o_f + o_b[:, ::-1]
    o = o * lax.rsqrt(jnp.mean(o * o, axis=-1, keepdims=True) + EPS)
    ret = o.reshape(B, T, RET_WIDTH).astype(p.dtype) * jax.nn.silu(p[..., G0:F0])
    four = fourier_mix(p[..., F0:CB0])
    conv = p[..., CB0:CC0] * dwconv3(p[..., CC0:CH0] * p[..., CH0:IN_WIDTH], conv_w)
    return jnp.concatenate([ret, four, conv], axis=-1), s_f, s_b

def conv_ffn(h, w_up, w_conv, w_down):
    u = dwconv3(h @ w_up, w_conv)
    val, gate = jnp.split(u, 2, axis=-1)
    return (val * jax.nn.silu(gate)) @ w_down

def setup_inputs(seed: int = 0) -> dict:
    key = jax.random.key(seed)
    ks = jax.random.split(key, 14)
    f32 = jnp.float32

    def nrm(k, shape, scale):
        return jax.random.normal(k, shape, f32) * scale

    base = np.log(2.0 ** (5.0 + np.arange(RET_HEADS)) - 1.0).astype(np.float32)
    return {
        'x': nrm(ks[0], (BATCH, SEQ, D_MODEL), 1.0),
        'c': nrm(ks[1], (BATCH, D_MODEL), 1.0),
        'ctx': nrm(ks[2], (BATCH, CTX_LEN, D_MODEL), 1.0),
        'c_ctx': nrm(ks[3], (D_MODEL,), 1.0),
        'w_mod': nrm(ks[4], (DEPTH, D_MODEL, 6 * D_MODEL), D_MODEL ** -0.5),
        'b_mod': nrm(ks[5], (DEPTH, 6 * D_MODEL), 0.02),
        'w_in': nrm(ks[6], (DEPTH, D_MODEL, IN_WIDTH), D_MODEL ** -0.5),
        'ret_decay_logit': jnp.asarray(base) + nrm(ks[7], (DEPTH, 2, RET_HEADS), 0.1),
        'mix_conv_w': nrm(ks[8], (DEPTH, 3, CONV_WIDTH), 3 ** -0.5),
        'w_out': nrm(ks[9], (DEPTH, MIX_WIDTH, D_MODEL), MIX_WIDTH ** -0.5),
        'ffn_w_up': nrm(ks[10], (DEPTH, D_MODEL, 2 * FFN_HIDDEN), D_MODEL ** -0.5),
        'ffn_conv_w': nrm(ks[11], (DEPTH, 3, 2 * FFN_HIDDEN), 3 ** -0.5),
        'ffn_w_down': nrm(ks[12], (DEPTH, FFN_HIDDEN, D_MODEL), FFN_HIDDEN ** -0.5),
        'final_norm_g': 1.0 + nrm(ks[13], (D_MODEL,), 0.05),
    }

def reference(x, c, ctx, c_ctx, w_mod, b_mod, w_in, ret_decay_logit, mix_conv_w, w_out,
              ffn_w_up, ffn_conv_w, ffn_w_down, final_norm_g):
    B, T, _ = x.shape
    Bc, Lc, _ = ctx.shape
    rope = axial_rope(T)
    zero_state = jnp.zeros((Bc, RET_HEADS, RET_HEAD_DIM, RET_HEAD_DIM), jnp.float32)
    silu_c = jax.nn.silu(c)
    silu_cc = jax.nn.silu(c_ctx)
    for l in range(DEPTH):
        last = l == DEPTH - 1
        sh1, sc1, g1, sh2, sc2, g2 = jnp.split((silu_c @ w_mod[l] + b_mod[l])[:, None, :], 6, axis=-1)
        csh1, csc1, cg1, csh2, csc2, cg2 = jnp.split(silu_cc @ w_mod[l] + b_mod[l], 6)
        log_decay = jax.nn.log_sigmoid(ret_decay_logit[l].astype(jnp.float32))

        hc = rmsnorm(ctx) * (1 + csc1) + csh1
        if last:
            kv = hc @ w_in[l][:, K0:G0]
            kc = _heads(kv[..., :RET_WIDTH], Bc, Lc) * RET_HEAD_DIM ** -0.5
            vc = _heads(kv[..., RET_WIDTH:], Bc, Lc)
            st_f = _chunk_states(_to_chunks(kc), _to_chunks(vc), log_decay[0], zero_state)[1]
            st_b = _chunk_states(_to_chunks(kc[:, ::-1]), _to_chunks(vc[:, ::-1]), log_decay[1], zero_state)[1]
        else:
            y_c, st_f, st_b = token_mixers(hc @ w_in[l], log_decay[0], log_decay[1],
                                           zero_state, zero_state, mix_conv_w[l], None)

        hx = rmsnorm(x) * (1 + sc1) + sh1
        y_x, _, _ = token_mixers(hx @ w_in[l], log_decay[0], log_decay[1],
                                 st_f, st_b, mix_conv_w[l], rope)
        x = x + g1 * (y_x @ w_out[l])
        x = x + g2 * conv_ffn(rmsnorm(x) * (1 + sc2) + sh2, ffn_w_up[l], ffn_conv_w[l], ffn_w_down[l])

        if not last:
            ctx = ctx + cg1 * (y_c @ w_out[l])
            ctx = ctx + cg2 * conv_ffn(rmsnorm(ctx) * (1 + csc2) + csh2, ffn_w_up[l], ffn_conv_w[l], ffn_w_down[l])
    return rmsnorm(x, final_norm_g)


_drawn_inputs = setup_inputs


def setup_inputs(seed=0):
    import zlib

    import numpy as np

    out = dict(_drawn_inputs(seed))
    spreads = {}
    factors = {}
    for name, (base, spread) in spreads.items():
        noise = np.random.default_rng([zlib.crc32(name.encode()), seed]).standard_normal(out[name].shape)
        drawn = base * np.exp(spread * noise) if base else spread * noise
        out[name] = __import__('jax').numpy.asarray(drawn.astype(out[name].dtype))
    for name, factor in factors.items():
        out[name] = (out[name] * factor).astype(out[name].dtype)
    return out
```

```python
import concourse.bass as bass
from concourse import mybir
from concourse.alu_op_type import AluOpType as ALU
import numpy as np

P = 128
T, C = 512, 256
TC = T + C
D = 1024
KB = D // P
DEPTH = 2
H, HD = 8, 64
HB = H * HD // P
CH = 128
NLC, NCC = T // CH, C // CH
FB = 256 // P
FG = 64
HID = 2816
NHB = HID // P
GROUPS = [8, 7, 7]
EPS = 1e-6
GRID_W = 64
ROPE_BASE = 10000.0
SH1, SC1, G1, SH2, SC2, G2 = range(6)
Y_ORDER = [4, 5, 6, 7, 0, 1, 2, 3]


def dft_slabs(layer):
    return NLC + (NCC if layer == 0 else 0)


def stream_plan():
    at, plan = 0, {}
    for l in range(DEPTH):
        for name, n in (("kv", 2 * HB), ("q", HB), ("cch", 2 * FB), ("cbf", 2 * FB), ("dft", dft_slabs(l)),
                        ("g", HB), ("out", KB)):
            plan[l, name] = at
            at += n
        for g, n in enumerate(GROUPS):
            plan[l, "up", g] = at
            at += 2 * n
            plan[l, "down", g] = at
            at += KB
    plan["end"] = at
    return plan


PLAN = stream_plan()


def pair_uses(s):
    return (s - sum(dft_slabs(l) for l in range(DEPTH) if PLAN[l, "dft"] < s)) // 2


MOD_ORDER = ([(0, k, b) for k in (SC1, SH1, G1, SH2, SC2, G2) for b in range(KB)]
             + [(1, k, b) for k in (SC1, SH1, G1, SH2, SC2, G2) for b in range(KB)])
MOD_START = 2 * KB
MODS_KV, MODS_Q, MODS_CCH, MODS_CBF = 4, 8, 3, 3
MODS_UP = 2
MOD_KIND = [SC1, SH1, G1, SH2, SC2, G2]


def mod_col(l, kind, b=0):
    return (l * 6 + MOD_KIND.index(kind)) * KB + b


def retention_plan(l):
    c0, c1 = NLC, NLC + 1
    items = [("state", 1, c1, None, ("b", 2)), ("state", 1, c0, ("b", 2), ("b", 3)),
             ("state", 0, c0, None, ("f", 0)), ("state", 0, c1, ("f", 0), ("f", 1))]
    if l == 0:
        items += [("chunk", c0, T, None, ("b", 2)), ("chunk", c1, T + CH, ("f", 0), None)]
    for c in range(NLC - 1, 0, -1):
        items.append(("state", 1, c, ("b", c), ("b", c - 1)))
    for c in range(NLC):
        items.append(("chunk", c, c * CH, ("f", (c + 1) % 2), ("b", c)))
        if c < NLC - 1:
            items.append(("state", 0, c, ("f", (c + 1) % 2), ("f", c % 2)))
    return items


def build_program(nc, io):
    fp32, f32r = mybir.dt.float32, mybir.dt.float32r
    ACT = mybir.ActivationFunctionType

    top = [(nc.sbuf_base + 63) // 64 * 64]

    def at(name, shape, offset, dt=fp32):
        return nc.alloc_sbuf_tensor_at(name, shape, dt, offset=offset)

    def new(name, shape, dt=fp32):
        t = at(name, shape, top[0], dt)
        top[0] += (int(np.prod(shape[1:])) * 4 + 31) // 32 * 32
        return t

    x = new("x", [P, KB, TC])
    h_hi = new("h_hi", [P, KB, TC], f32r)
    h_lo = new("h_lo", [P, KB, TC], f32r)
    raw = [new(f"raw{i}", [P, 8 * P]) for i in range(2)]
    w_hi = [new(f"w_hi{i}", [P, 8 * P], f32r) for i in range(2)]
    w_lo = [new(f"w_lo{i}", [P, 8 * P], f32r) for i in range(2)]
    mask = new("mask", [P, 2, 4, CH])
    xi = new("xi", [P, 2, HB, CH])
    rope_cos = new("rope_cos", [P, T])
    rope_sin = new("rope_sin", [P, T])
    expo = new("expo", [P, 6, CH])
    ident = new("ident", [P, P])
    chan = new("chan", [P, 2 * P])
    small = new("small", [P, 4])
    eps = new("eps", [P, 1])
    ones = new("ones", [P, 1])
    n_mod = len(MOD_ORDER)
    modv = new("modv", [P, 2, n_mod])
    mod_acc = new("mod_acc", [P, 2, 2])
    vec_w = {"bmod": n_mod, "ffnw": DEPTH * 2 * NHB * 3, "mixw": DEPTH * FB * 3, "fng": KB, "logit": DEPTH * 24}
    vec_at, n = {}, 0
    for k, v in vec_w.items():
        vec_at[k] = n
        n += v
    vecs = new("vecs", [P, n])
    ld = new("ld", [P, DEPTH * 24])
    ldt = new("ldt", [P, 3, DEPTH * 24])
    zeta = new("zeta", [P, 2, H])
    cdec = new("cdec", [P, 2, HB])
    rs = new("rs", [P, 8])
    rinv = new("rinv", [P, 8])
    work = top[0]
    assert work + 92160 <= nc.sbuf_usable_end, (work + 92160, nc.sbuf_usable_end)

    Y = at("Y", [P, KB, TC], work)
    kT = at("kT", [P, HB, TC], work + 24576)
    ktok = at("ktok", [P, NLC + NCC, 4 * P], work + 36864)
    vtok = at("vtok", [P, NLC + NCC, 4 * P], work + 49152)
    z = at("z", [P, FB, TC], work + 61440)
    state = {"b": at("S_b", [P, NLC, HB, P], work + 67584), "f": at("S_f", [P, 2, HB, P], work + 75776)}
    St = at("St", [P, 2, 4, CH], work + 79872)
    osq = at("osq", [P, HB, CH], work + 83968)
    vz = at("vz", [P, H, HD], work + 86016)
    qxi = at("qxi", [P, 2, HB, CH], work + 88064)
    c_b = at("c_b", [P, 2, D], work + 67584)
    mod_slot = [at(f"mod_slot{i}", [P, D], work + 75776 + 4096 * i) for i in range(2)]
    rot = [at(f"rot{i}", [P, T], work + 83968 + 2048 * i) for i in range(2)]
    eb = at("eb", [P, 2, 4, CH], work + 88064)
    G_hi = at("G_hi", [P, NLC, 4 * P], work + 24576, f32r)
    G_lo = at("G_lo", [P, NLC, 4 * P], work + 32768, f32r)
    ct = at("ct", [P, TC], work + 88064)
    sg = [at(f"sg{i}", [P, TC], work + 44032 + 3072 * i) for i in range(2)]
    hid_hi = at("hid_hi", [P, max(GROUPS), TC], work, f32r)
    hid_lo = at("hid_lo", [P, max(GROUPS), TC], work + 24576, f32r)
    tv = at("tv", [P, TC], work + 49152)
    tg = at("tg", [P, TC], work + 52224)
    sq = [at(f"sq{i}", [P, TC], work + 61440 + 3072 * i) for i in range(2)]
    nt = [at(f"nt{i}", [P, TC], work + 83968 + 3072 * i) for i in range(2)]
    fin = at("fin", [P, KB, T], work)
    start_slot = [at(f"start_slot{i}", [P, 2, D], work + (8192 * i if i < 7 else 75776)) for i in range(8)]

    pair = [nc.alloc_psum_tensor(f"pair{i}", [P, 1024], fp32) for i in range(2)]
    aux01 = nc.alloc_psum_tensor("aux01", [P, 1024], fp32)
    aux23 = nc.alloc_psum_tensor("aux23", [P, 1024], fp32)

    def aux(i):
        return (aux01 if i < 2 else aux23)[:, (i % 2) * 512:(i % 2) * 512 + 512]

    def by_block(bank):
        return bank.rearrange("p (b i) -> p b i", b=HB)

    sem = nc.alloc_semaphore

    def vec(name, i):
        return vecs[:, vec_at[name] + i:vec_at[name] + i + 1]

    def vec_dyn(name, i):
        return vecs[:, bass.ds(i + vec_at[name], 1)]

    def mod(l, st, kind, b):
        i = mod_col(l, kind, b)
        return modv[:, st, i:i + 1]

    loaded = [sem(f"slab_loaded{i}") for i in range(2)]
    split = sem("slab_split")
    done = sem("slab_done")
    drained = [sem(f"pair_drained{i}") for i in range(2)]
    c_loaded, c_ready = sem("c_loaded"), sem("c_ready")
    x_loaded = [sem(f"x_loaded{i}") for i in range(4)]
    consts_loaded = sem("consts_loaded")
    start_loaded = [sem(f"start_mods_loaded{i}") for i in range(8)]
    mod_loaded = [sem(f"mod_loaded{i}") for i in range(2)]
    mod_used, mods_ready = sem("mod_used"), sem("mods_ready")
    fills = sem("fills_done")
    out_ready, out_stored = sem("out_ready"), sem("out_stored")
    rot_loaded = [sem(f"rot_loaded{i}") for i in range(2)]
    ld_ready = sem("ld_ready")
    dve_chain = sem("dve_chain")

    S = []
    for l in range(DEPTH):
        names = ["decay_exp", "decay_ready", "roped", "tr_done", "v_moved", "k_moved", "conv_done", "vz_ready",
                 "u_done", "state_ready", "qxi_ready", "scores_done", "St_ready", "o_done", "o_copied", "osq_ready",
                 "hsum_done", "hrs_ready", "hrinv_ready", "hbc_done", "o_ready", "G_done", "G_hi_ready", "G_split",
                 "four_ready", "y_ready", "y_hi", "y_split", "tv_ready", "tg_ready", "silu_ready",
                 "p_ready", "hid_hi_ready", "hid_ready"] + (["x1_ctx", "x2_ctx"] if l == 0 else [])
        S.append({n: sem(f"{n}_{l}") for n in names})
    norms = {n: {k: sem(f"{k}_{n}") for k in ("sq_ready", "sq_used", "rs_ready", "rinv_ready", "rbc_ready",
                                             "nt_ready", "hi_ready", "h_ready")}
             for n in ("n1_0", "n2_0", "n1_1", "n2_1", "final")}

    def layer_cols(l):
        return [(0, 0, T), (1, T, TC)] if l == 0 else [(0, 0, T)]

    def drained_by(s):
        even = s - s % 2
        return drained[s % 2], pair_uses(even) + 1

    block = nc.Block()
    with block:
        @block.sync
        def _(sp):
            for i, name in enumerate(("c", "c_ctx")):
                sp.dma_start(c_b[:, i, :], io[name].to_broadcast([P, D])).then_inc(c_loaded, 16)

            def load_slab(s, p):
                sp.dma_start(raw[p][:, :], io["slabs"][s, :, :]).then_inc(loaded[p], 16)

            def load_slabs(first, n):
                with sp.Fori(0, n) as i:
                    for p in range(2):
                        sp.wait_ge(split, 2 * (first + p - 1) + 4 * i)
                        load_slab(first + p + 2 * i, p)

            def load_mods(m, n):
                for j in range(m, m + n):
                    if j >= 2:
                        sp.wait_ge(mod_used, j - 1)
                    sp.dma_start(mod_slot[j % 2][:, :], io["mods"][MOD_START + j, :, :]).then_inc(mod_loaded[j % 2], 16)

            for i in range(8):
                sp.dma_start(start_slot[i][:, :, :], io["mods"][2 * i:2 * i + 2, :, :].rearrange("s p n -> p s n"))\
                    .then_inc(start_loaded[i], 16)
            load_slab(0, 0)
            load_slab(1, 1)
            sp.wait_ge(mods_ready, 1)
            s, m = 2, 0
            for n_mods in [MODS_KV] * HB + [MODS_Q // 2] * (HB // 2) + [MODS_CCH] * FB + [MODS_CBF] * FB:
                load_slabs(s, 1)
                load_mods(m, n_mods)
                s, m = s + 2, m + n_mods
            load_slabs(s, (PLAN[0, "up", 0] - s) // 2)
            for g, n in enumerate(GROUPS):
                s = PLAN[0, "up", g]
                load_slabs(s, 1)
                with sp.Fori(0, n - 1) as i:
                    for p in range(2):
                        sp.wait_ge(split, 2 * (s + 1 + p) + 4 * i)
                        load_slab(s + 2 + p + 2 * i, p)
                    for p in range(MODS_UP):
                        sp.wait_ge(mod_used, m + p - 1 + 2 * i)
                        sp.dma_start(mod_slot[p][:, :], io["mods"][2 * i + (MOD_START + m + p), :, :])\
                            .then_inc(mod_loaded[p], 16)
                m += (n - 1) * MODS_UP
                load_mods(m, MODS_UP)
                m += MODS_UP
                load_slabs(PLAN[0, "down", g], KB // 2)
            assert MOD_START + m == n_mod
            load_slabs(PLAN[1, "kv"], (PLAN["end"] - PLAN[1, "kv"]) // 2)
            for k in range(KB):
                sp.wait_ge(out_ready, k + 1)
                sp.dma_start(io["out"][k, :, :], fin[:, k, :]).then_inc(out_stored, 16)
            sp.wait_ge(out_stored, 16 * KB)

        @block.gpsimd
        def _(pool):
            nc.gpsimd.memset(eps[:, :], EPS).then_inc(fills, 1)
            nc.gpsimd.memset(ones[:, :], 1.0).then_inc(fills, 1)

            pool.wait_ge(fills, 2)

            def split_slab(p, n, first):
                pool.wait_ge(loaded[p], 16 * (n + 1))
                if not first:
                    pool.wait_ge(done, 2 * n + (p - 1))
                nc.gpsimd.tensor_tensor(w_hi[p][:, :], raw[p][:, :], ones[:, 0:1].to_broadcast([P, 8 * P]),
                                        ALU.mult).then_inc(split, 1)
                pool.wait_ge(split, 4 * n + (2 * p + 1))
                nc.gpsimd.tensor_tensor(w_lo[p][:, :], raw[p][:, :], w_hi[p][:, :].bitcast(fp32),
                                        ALU.subtract).then_inc(split, 1)
            for p in range(2):
                split_slab(p, 0, True)
            with pool.Fori(1, PLAN["end"] // 2) as i:
                for p in range(2):
                    split_slab(p, i, False)

        @block.scalar
        def _(act):
            for i in range(4):
                act.dma_start(x[:, 2 * i:2 * i + 2, :], io["x"][:, 2 * i:2 * i + 2, :]).then_inc(x_loaded[i], 16)
            tab = io["tables"]
            for dst, src in ((vecs[:, :], io["vecs"]), (rope_cos[:, :], tab[:, 0:T]), (rope_sin[:, :], tab[:, T:2 * T]),
                             (expo[:, :, :].rearrange("p a b -> p (a b)"), tab[:, 2 * T:2 * T + 6 * CH]),
                             (ident[:, :], tab[:, 1792:1920]), (chan[:, :], tab[:, 1920:2176]),
                             (small[:, :], tab[:, 2176:2180])):
                act.dma_start(dst, src).then_inc(consts_loaded, 16)
            act.wait_ge(c_loaded, 32)
            nc.scalar.activation(c_b[:, :, :], c_b[:, :, :], ACT.Silu).then_inc(c_ready, 1)
            act.wait_ge(fills, 2)
            act.wait_ge(consts_loaded, 16 * 7)
            act.wait_ge(ld_ready, 1)
            nc.scalar.activation(ldt[:, 0, :], ldt[:, 1, :], ACT.Exp, scale=-1.0).then_inc(ld_ready, 1)
            act.wait_ge(ld_ready, 3)

            def decays(l):
                s, o = S[l], l * 24
                if l:
                    act.wait_ge(S[0]["hid_ready"], NHB)
                for d, dst in ((0, mask), (1, eb)):
                    for hh in range(H):
                        nc.scalar.activation(dst[:, hh % 2, hh // 2, :], expo[:, 2 * d, :], ACT.Exp,
                                             scale=ld[:, o + 8 * d + hh:o + 8 * d + hh + 1]).then_inc(s["decay_exp"], 1)
                for d in range(2):
                    for b in range(HB):
                        q = o + 16 + 4 * d + b
                        nc.scalar.activation(xi[:, d, b, :], expo[:, 4 + d, :], ACT.Exp, scale=ld[:, q:q + 1])\
                            .then_inc(s["decay_exp"], 1)
                    nc.scalar.activation(zeta[:, d, :], ld[:, o + 8 * d:o + 8 * d + 8], ACT.Exp,
                                         scale=small[:, 2 + d:3 + d]).then_inc(s["decay_exp"], 1)
                nc.scalar.activation(cdec[:, :, :].rearrange("p a b -> p (a b)"), ld[:, o + 16:o + 24], ACT.Exp,
                                     scale=float(CH)).then_inc(s["decay_exp"], 1)

            def norm(name, ncol, l, sh, x_ready):
                s = norms[name]
                for k in range(KB):
                    x_ready(k)
                    if k >= 2:
                        act.wait_ge(s["sq_used"], k - 1)
                    nc.scalar.activation(sq[k % 2][:, 0:ncol], x[:, k, 0:ncol], ACT.Square).then_inc(s["sq_ready"], 1)
                act.wait_ge(s["sq_used"], KB)
                nc.scalar.activation(rs[:, 0:ncol // P], aux(2)[:, 0:ncol // P], ACT.Sqrt, bias=eps[:, 0:1],
                                     scale=1.0 / D).then_inc(s["rs_ready"], 1)
                if sh is None:
                    return
                cols = [(0, 0, T)] + ([(1, T, TC)] if ncol == TC else [])
                for k in range(KB):
                    for st, a, b in cols:
                        act.wait_ge(s["nt_ready"], len(cols) * k + st + 1)
                        nc.scalar.activation(h_hi[:, k, a:b], nt[k % 2][:, a:b], ACT.Identity,
                                             bias=mod(l, st, sh, k)).then_inc(s["hi_ready"], 1)

            def x_after(first_slab, ctx):
                def ready(k):
                    act.wait_ge(*drained_by(first_slab + k))
                    if ctx is not None:
                        act.wait_ge(ctx[0], ctx[1] + k + 1)
                return ready

            for l in range(DEPTH):
                s = S[l]
                cols = layer_cols(l)
                nlat = cols[-1][2]
                decays(l)
                if l == 0:
                    norm("n1_0", TC, 0, SH1, lambda k: act.wait_ge(x_loaded[k // 2], 16))
                else:
                    norm("n1_1", TC, 1, SH1, x_after(PLAN[0, "down", 2], (S[0]["x2_ctx"], 2 * KB)))

                def copy_out(slab, dst, ncol):
                    p = slab % 2
                    act.wait_ge(done, slab + 1)
                    nc.scalar.activation(dst, pair[p][:, 0:ncol], ACT.Copy).then_inc(drained[p], 1)

                def swap(src, slab, unit):
                    p = unit % 2
                    act.wait_ge(*drained_by(slab))
                    if unit >= 2:
                        act.wait_ge(s["roped"], unit - 1)
                    for g in range(4):
                        a, b = 32 * g, 32 * (g ^ 1)
                        act.dma_start(rot[p][a:a + 32, :], src[b:b + 32]).then_inc(rot_loaded[p], 16)

                kv, q0 = PLAN[l, "kv"], PLAN[l, "q"]
                for j in range(HB):
                    copy_out(kv + 2 * j, kT[:, j, :], TC)
                    swap(kT[:, j, 0:T], kv + 2 * j, j)
                    copy_out(kv + 2 * j + 1, Y[:, j, :], TC)
                for c in range(NLC + NCC):
                    act.wait_ge(s["tr_done"], c + 1)
                    nc.scalar.activation(vtok[:, c, :], aux(2 + c % 2), ACT.Copy).then_inc(s["v_moved"], 1)
                for j in range(HB):
                    copy_out(q0 + j, Y[:, j, 0:nlat], nlat)
                    swap(Y[:, j, 0:T], q0 + j, HB + j)
                for b in range(FB):
                    copy_out(PLAN[l, "cch"] + 2 * b, z[:, b, 0:nlat], nlat)
                for b in range(FB):
                    copy_out(PLAN[l, "cbf"] + 2 * b, Y[:, 6 + b, 0:nlat], nlat)
                    copy_out(PLAN[l, "cbf"] + 2 * b + 1, Y[:, 4 + b, 0:nlat], nlat)
                n = 0
                for item in retention_plan(l):
                    if item[0] != "chunk":
                        continue
                    _, c, col, _, _ = item
                    act.wait_ge(s["o_done"], n + 1)
                    nc.scalar.activation(Y[:, 0:HB, col:col + CH], by_block(aux(2)), ACT.Copy).then_inc(s["o_copied"], 1)
                    nc.scalar.activation(osq[:, :, :], by_block(aux(2)), ACT.Square).then_inc(s["osq_ready"], 1)
                    act.wait_ge(s["hsum_done"], n + 1)
                    nc.scalar.activation(rs[:, 0:H], aux(3)[:, 0:H], ACT.Sqrt, bias=eps[:, 0:1], scale=1.0 / HD)\
                        .then_inc(s["hrs_ready"], 1)
                    n += 1
                if l == 0:
                    act.wait_ge(s["o_ready"], n)
                    for i, name in enumerate(("c", "c_ctx")):
                        act.dma_start(c_b[:, i, :], io[name].to_broadcast([P, D])).then_inc(c_loaded, 16)
                for n in range(dft_slabs(l)):
                    act.wait_ge(s["G_done"], n + 1)
                    if n >= NLC:
                        act.wait_ge(done, PLAN[l, "dft"] + n - NLC + 1)
                    nc.scalar.activation(G_hi[:, n % NLC, :], aux(n % 2), ACT.Copy).then_inc(s["G_hi_ready"], 1)
                for j in range(HB):
                    g = PLAN[l, "g"] + j
                    act.wait_ge(done, g + 1)
                    if j >= 2:
                        act.wait_ge(s["y_ready"], j - 1)
                    nc.scalar.activation(sg[j % 2][:, 0:nlat], pair[j % 2][:, 0:nlat], ACT.Silu)\
                        .then_inc(drained[j % 2], 1)
                if l == 0:
                    act.wait_ge(c_loaded, 64)
                    nc.scalar.activation(c_b[:, :, :], c_b[:, :, :], ACT.Silu).then_inc(c_ready, 1)
                act.wait_ge(done, PLAN[l, "out"])
                for k in Y_ORDER:
                    if k < HB:
                        act.wait_ge(s["y_ready"], k + 1)
                    elif k == 4:
                        act.wait_ge(s["four_ready"], FB * (2 if l == 0 else 1))
                    elif k == 6:
                        act.wait_ge(s["conv_done"], FB)
                    nc.scalar.activation(h_hi[:, k, 0:nlat], Y[:, k, 0:nlat], ACT.Copy).then_inc(s["y_hi"], 1)
                norm(f"n2_{l}", nlat, l, SH2, x_after(PLAN[l, "out"], (s["x1_ctx"], 0) if l == 0 else None))
                u = 0
                for g, n in enumerate(GROUPS):
                    s0 = PLAN[l, "up", g]

                    def hidden(i, first):
                        act.wait_ge(done, s0 + 1 + 2 * i)
                        if not first:
                            act.wait_ge(s["hid_ready"], u + i)
                        w = (l * 2 * NHB + u) * 3 + 1 + 3 * i
                        nc.scalar.activation(tv[:, 0:nlat], pair[0][:, 0:nlat], ACT.Copy, scale=vec_dyn("ffnw", w))\
                            .then_inc(s["tv_ready"], 1)
                        act.wait_ge(done, s0 + 2 + 2 * i)
                        nc.scalar.activation(tg[:, 0:nlat], pair[1][:, 0:nlat], ACT.Copy,
                                             scale=vec_dyn("ffnw", w + 3 * NHB)).then_inc(s["tg_ready"], 1)
                        act.wait_ge(drained[1], pair_uses(s0) + 1 + i)
                        nc.scalar.activation(tg[:, 0:nlat], tg[:, 0:nlat], ACT.Silu).then_inc(s["silu_ready"], 1)
                        act.wait_ge(s["p_ready"], u + 1 + i)
                        nc.scalar.activation(hid_hi[:, i, 0:nlat], tv[:, 0:nlat], ACT.Copy)\
                            .then_inc(s["hid_hi_ready"], 1)
                    hidden(0, u == 0)
                    with act.Fori(1, n) as i:
                        hidden(i, False)
                    u += n
            norm("final", T, 0, None, x_after(PLAN[1, "down", 2], None))

        @block.vector
        def _(dve):
            steps = [0]

            def chain(ins, base=None):
                steps[0] += 1
                ins.then_inc(dve_chain, 1)
                dve.wait_ge(dve_chain, steps[0] if base is None else base + steps[0])

            def mod_dots(slab, col, acc, used):
                for st in range(2):
                    chain(nc.vector.tensor_tensor_reduce(out=aux01[:, :], in0=slab, in1=c_b[:, st, :], scale=1.0,
                                                         scalar=0.0, op0=ALU.mult, op1=ALU.add,
                                                         accum_out=mod_acc[:, acc, st:st + 1]), mod_dots.base)
                nc.vector.tensor_tensor(modv[:, :, bass.ds(col, 1)], mod_acc[:, acc, :].unsqueeze(2),
                                        vec_dyn("bmod", col).unsqueeze(1).to_broadcast([P, 2, 1]), ALU.add)\
                    .then_inc(used, 1)
            mod_dots.base = None

            def ring_mods(m, n):
                for j in range(m, m + n):
                    dve.wait_ge(mod_loaded[j % 2], 16 * (j // 2 + 1))
                    mod_dots(mod_slot[j % 2][:, :], MOD_START + j, j % 2, mod_used)

            def one_plus(l, kind, ready):
                c = mod_col(l, kind)
                nc.vector.tensor_scalar(modv[:, :, c:c + KB], modv[:, :, c:c + KB], 1.0, None, ALU.add).then_inc(ready, 1)

            dve.wait_ge(fills, 2)
            dve.wait_ge(consts_loaded, 16 * 7)
            lg = vecs[:, vec_at["logit"]:vec_at["logit"] + DEPTH * 24]
            ya, yb, yc = ldt[:, 0, :], ldt[:, 1, :], ldt[:, 2, :]
            chain(nc.vector.tensor_scalar(yb, lg, -1.0, None, ALU.mult))
            nc.vector.tensor_tensor(yb, yb, lg, ALU.max).then_inc(ld_ready, 1)
            dve.wait_ge(ld_ready, 2)
            chain(nc.vector.tensor_scalar(yb, ya, 2.0, None, ALU.add))
            chain(nc.vector.reciprocal(yb, yb))
            chain(nc.vector.tensor_tensor(ya, ya, yb, ALU.mult))
            chain(nc.vector.tensor_tensor(yb, ya, ya, ALU.mult))
            chain(nc.vector.tensor_scalar(yc, yb, 1.0 / 17, None, ALU.mult))
            for k in range(15, 1, -2):
                chain(nc.vector.scalar_tensor_tensor(yc, yc, 1.0 / k, yb, ALU.add, ALU.mult))
            chain(nc.vector.scalar_tensor_tensor(yc, yc, 1.0, ya, ALU.add, ALU.mult))
            chain(nc.vector.tensor_scalar(yb, lg, 0.0, None, ALU.min))
            nc.vector.scalar_tensor_tensor(ld[:, :], yc, -2.0, yb, ALU.mult, ALU.add).then_inc(ld_ready, 1)

            dve.wait_ge(c_ready, 1)
            for i in range(MOD_START):
                dve.wait_ge(start_loaded[i // 2], 16)
                mod_dots(start_slot[i // 2][:, i % 2, :], i, i % 2, dve_chain)
                steps[0] += 1
            dve.wait_ge(dve_chain, steps[0])
            one_plus(0, SC1, mods_ready)

            def decays(l):
                s = S[l]
                dve.wait_ge(s["decay_exp"], 27)
                for p in range(2):
                    chain(nc.vector.tensor_tensor(mask[:, p, :, :], mask[:, p, :, :],
                                                  expo[:, 1:2, :].to_broadcast([P, 4, CH]), ALU.mult))
                    chain(nc.vector.tensor_tensor(eb[:, p, :, :], eb[:, p, :, :],
                                                  expo[:, 3:4, :].to_broadcast([P, 4, CH]), ALU.mult))
                    chain(nc.vector.tensor_tensor(mask[:, p, :, :], mask[:, p, :, :], eb[:, p, :, :], ALU.add))
                chain(nc.vector.tensor_scalar(zeta[:, :, :], zeta[:, :, :], HD ** -0.5, None, ALU.mult))

            def norm(name, ncol, l, sc, sh):
                s = norms[name]
                cols = [(0, 0, T)] + ([(1, T, TC)] if ncol == TC else [])
                dve.wait_ge(s["rs_ready"], 1)
                nc.vector.reciprocal(rinv[:, 0:ncol // P], rs[:, 0:ncol // P]).then_inc(s["rinv_ready"], 1)
                dve.wait_ge(s["rbc_ready"], 1)

                def scale(k):
                    for st, a, b in cols:
                        nc.vector.scalar_tensor_tensor(nt[k % 2][:, a:b], aux23[:, a:b], mod(l, st, sc, k),
                                                       x[:, k, a:b], ALU.mult, ALU.mult).then_inc(s["nt_ready"], 1)

                if sc is None:
                    for k in range(KB):
                        nc.vector.scalar_tensor_tensor(fin[:, k, :], aux23[:, 0:T], vec("fng", k), x[:, k, 0:T],
                                                       ALU.mult, ALU.mult).then_inc(out_ready, 1)
                    return
                scale(0)
                for k in range(KB):
                    if k + 1 < KB:
                        if k:
                            dve.wait_ge(s["h_ready"], len(cols) * k)
                        scale(k + 1)
                    for st, a, b in cols:
                        dve.wait_ge(s["hi_ready"], len(cols) * k + st + 1)
                        nc.vector.scalar_tensor_tensor(h_lo[:, k, a:b], nt[k % 2][:, a:b], mod(l, st, sh, k),
                                                       h_hi[:, k, a:b].bitcast(fp32), ALU.add, ALU.subtract)\
                            .then_inc(s["h_ready"], 1)

            m = 0
            for l in range(DEPTH):
                s = S[l]
                cols = layer_cols(l)
                nlat = cols[-1][2]
                decays(l)
                if l == 0:
                    dve.wait_ge(mods_ready, 1)
                norm(f"n1_{l}", TC, l, SC1, SH1)

                def rope(buf, unit):
                    p = unit % 2
                    dve.wait_ge(rot_loaded[p], 64 * (l * HB + unit // 2 + 1))
                    chain(nc.vector.tensor_tensor(rot[p][:, :], rot[p][:, :], rope_sin[:, :], ALU.mult))
                    chain(nc.vector.tensor_tensor(buf, buf, rope_cos[:, :], ALU.mult))
                    nc.vector.tensor_tensor(buf, buf, rot[p][:, :], ALU.add).then_inc(s["roped"], 1)

                for j in range(HB):
                    rope(kT[:, j, 0:T], j)
                    if l == 0:
                        ring_mods(m, MODS_KV)
                        m += MODS_KV
                for c in range(NLC + NCC):
                    u = NLC + NCC + c
                    dve.wait_ge(s["tr_done"], u + 1)
                    nc.vector.tensor_copy(ktok[:, c, :], aux(2 + u % 2)).then_inc(s["k_moved"], 1)
                for j in range(HB):
                    rope(Y[:, j, 0:T], HB + j)
                    if l == 0 and j % 2:
                        ring_mods(m, MODS_Q // 2)
                        m += MODS_Q // 2
                for b in range(FB):
                    slab = PLAN[l, "cch"] + 2 * b
                    dve.wait_ge(*drained_by(slab))
                    dve.wait_ge(done, slab + 2)
                    nc.vector.tensor_tensor(z[:, b, 0:nlat], pair[1][:, 0:nlat], z[:, b, 0:nlat], ALU.mult)\
                        .then_inc(drained[1], 1)
                    if l == 0:
                        ring_mods(m, MODS_CCH)
                        m += MODS_CCH
                for b in range(FB):
                    w = [vec("mixw", (l * FB + b) * 3 + t) for t in range(3)]
                    dve.wait_ge(*drained_by(PLAN[l, "cch"] + 2 * b + 1))
                    if b:
                        dve.wait_ge(s["conv_done"], b)
                    chain(nc.vector.tensor_scalar(ct[:, 0:nlat], z[:, b, 0:nlat], w[1], None, ALU.mult))
                    for _, a0, a1 in cols:
                        chain(nc.vector.scalar_tensor_tensor(ct[:, a0 + 1:a1], z[:, b, a0:a1 - 1], w[0],
                                                             ct[:, a0 + 1:a1], ALU.mult, ALU.add))
                        chain(nc.vector.scalar_tensor_tensor(ct[:, a0:a1 - 1], z[:, b, a0 + 1:a1], w[2],
                                                             ct[:, a0:a1 - 1], ALU.mult, ALU.add))
                    dve.wait_ge(*drained_by(PLAN[l, "cbf"] + 2 * b))
                    nc.vector.tensor_tensor(Y[:, 6 + b, 0:nlat], Y[:, 6 + b, 0:nlat], ct[:, 0:nlat], ALU.mult)\
                        .then_inc(s["conv_done"], 1)
                    if l == 0:
                        ring_mods(m, MODS_CBF)
                        m += MODS_CBF
                if l == 0:
                    dve.wait_ge(mod_used, m)
                    one_plus(0, SC2, mods_ready)
                    dve.wait_ge(mods_ready, 2)

                dve.wait_ge(s["conv_done"], FB)
                for t in state.values():
                    chain(nc.vector.memset(t[:, :, :, :], 0.0))
                n_state = n_chunk = 0
                for item in retention_plan(l):
                    if item[0] == "state":
                        _, d, c, prev, nxt = item
                        nc.vector.tensor_tensor(vz[:, :, :], vtok[:, c, :].rearrange("p (h e) -> p h e", h=H),
                                                zeta[:, d, :].unsqueeze(2).to_broadcast([P, H, HD]), ALU.mult)\
                            .then_inc(s["vz_ready"], 1)
                        n_state += 1
                        dve.wait_ge(s["u_done"], n_state)
                        to = state[nxt[0]][:, nxt[1], :, :]
                        for hh in range(2):
                            r = slice(HD * hh, HD * hh + HD)
                            U = by_block(aux(3))[r, :, r]
                            if prev is None:
                                nc.vector.tensor_copy(to[r, :, r], U).then_inc(s["state_ready"], 1)
                            else:
                                chain(nc.vector.tensor_tensor(to[r, :, r], state[prev[0]][r, prev[1], :, r],
                                                              cdec[r, d, :].unsqueeze(2).to_broadcast([HD, HB, HD]),
                                                              ALU.mult))
                                nc.vector.tensor_tensor(to[r, :, r], U, to[r, :, r], ALU.add)\
                                    .then_inc(s["state_ready"], 1)
                        dve.wait_ge(s["state_ready"], 2 * n_state)
                        continue
                    _, c, col, fwd, bwd = item
                    q = Y[:, 0:HB, col:col + CH]
                    for d, st in ((0, fwd), (1, bwd)):
                        nc.vector.tensor_tensor(qxi[:, d, :, :], q, xi[:, d, :, :], ALU.mult).then_inc(s["qxi_ready"], 1)
                    dve.wait_ge(s["scores_done"], n_chunk + 1)
                    for p in range(2):
                        nc.vector.tensor_tensor(St[:, p, :, :], by_block(aux(p)), mask[:, p, :, :], ALU.mult)\
                            .then_inc(s["St_ready"], 1)
                    dve.wait_ge(s["hrs_ready"], n_chunk + 1)
                    nc.vector.reciprocal(rinv[:, 0:H], rs[:, 0:H]).then_inc(s["hrinv_ready"], 1)
                    dve.wait_ge(s["hbc_done"], n_chunk + 1)
                    dve.wait_ge(s["o_copied"], n_chunk + 1)
                    nc.vector.tensor_tensor(q, by_block(aux(3)), q, ALU.mult).then_inc(s["o_ready"], 1)
                    n_chunk += 1
                dve.wait_ge(s["o_ready"], n_chunk)
                for n in range(dft_slabs(l)):
                    dve.wait_ge(s["G_hi_ready"], n + 1)
                    nc.vector.tensor_tensor(G_lo[:, n % NLC, :], aux(n % 2), G_hi[:, n % NLC, :].bitcast(fp32),
                                            ALU.subtract).then_inc(s["G_split"], 1)
                    if n == dft_slabs(l) - 1:
                        parts = [(NLC, 0, T)] + ([(NLC + NCC, T, TC)] if l == 0 else [])
                        for count, a0, a1 in parts:
                            dve.wait_ge(done, PLAN[l, "dft"] + count)
                            for b in range(FB):
                                nc.vector.tensor_copy(Y[:, 4 + b, a0:a1], aux(2 + b)[:, 0:a1 - a0])\
                                    .then_inc(s["four_ready"], 1)
                for j in range(HB):
                    dve.wait_ge(*drained_by(PLAN[l, "g"] + j))
                    nc.vector.tensor_tensor(Y[:, j, 0:nlat], Y[:, j, 0:nlat], sg[j % 2][:, 0:nlat], ALU.mult)\
                        .then_inc(s["y_ready"], 1)
                for n, k in enumerate(Y_ORDER):
                    dve.wait_ge(s["y_hi"], n + 1)
                    nc.vector.tensor_tensor(h_lo[:, k, 0:nlat], Y[:, k, 0:nlat], h_hi[:, k, 0:nlat].bitcast(fp32),
                                            ALU.subtract).then_inc(s["y_split"], 1)

                def residual(first, kind, ctx_ready, ctx_before=0):
                    c0 = mod_col(l, kind)
                    for p in range(2):
                        dve.wait_ge(drained[p], pair_uses(first))
                    if ctx_before:
                        dve.wait_ge(ctx_ready, ctx_before)
                    with dve.Fori(0, KB // 2) as i:
                        for p in range(2):
                            dve.wait_ge(done, first + p + 1 + 2 * i)
                            for st, a0, a1 in reversed(cols):
                                nc.vector.scalar_tensor_tensor(
                                    x[:, 2 * i + p, a0:a1], pair[p][:, a0:a1], modv[:, st, bass.ds(2 * i + (c0 + p), 1)],
                                    x[:, 2 * i + p, a0:a1], ALU.mult, ALU.add)\
                                    .then_inc(drained[p] if st == 0 else ctx_ready, 1)

                residual(PLAN[l, "out"], G1, s.get("x1_ctx"))
                norm(f"n2_{l}", nlat, l, SC2, SH2)
                if l == 0:
                    dve.wait_ge(c_ready, 2)
                u = 0
                for g, n in enumerate(GROUPS):
                    s0 = PLAN[l, "up", g]
                    per = 2 * (2 * len(cols) - 1) + (2 * MODS_UP if l == 0 else 0)
                    start = steps[0]
                    with dve.Fori(0, n) as i:
                        base = i * per

                        def outer_taps(t, p, w):
                            ops = []
                            for _, a0, a1 in cols:
                                ops += [(t[:, a0 + 1:a1], pair[p][:, a0:a1 - 1], 0),
                                        (t[:, a0:a1 - 1], pair[p][:, a0 + 1:a1], 2)]
                            for k, (dst, src, tap) in enumerate(ops):
                                ins = nc.vector.scalar_tensor_tensor(dst, src, vec_dyn("ffnw", w + tap), dst,
                                                                     ALU.mult, ALU.add)
                                if k < len(ops) - 1:
                                    chain(ins, base)
                                else:
                                    ins.then_inc(drained[p], 1)

                        w = (l * 2 * NHB + u) * 3 + 3 * i
                        dve.wait_ge(s["tv_ready"], u + 1 + i)
                        outer_taps(tv, 0, w)
                        dve.wait_ge(s["tg_ready"], u + 1 + i)
                        outer_taps(tg, 1, w + 3 * NHB)
                        dve.wait_ge(s["silu_ready"], u + 1 + i)
                        dve.wait_ge(drained[0], pair_uses(s0) + 1 + i)
                        nc.vector.tensor_tensor(tv[:, 0:nlat], tv[:, 0:nlat], tg[:, 0:nlat], ALU.mult)\
                            .then_inc(s["p_ready"], 1)
                        dve.wait_ge(s["hid_hi_ready"], u + 1 + i)
                        nc.vector.tensor_tensor(hid_lo[:, i, 0:nlat], tv[:, 0:nlat],
                                                hid_hi[:, i, 0:nlat].bitcast(fp32), ALU.subtract)\
                            .then_inc(s["hid_ready"], 1)
                        if l == 0:
                            mod_dots.base = base
                            for p in range(MODS_UP):
                                dve.wait_ge(mod_loaded[p], 16 * (m // 2 + 1) + 16 * i)
                                mod_dots(mod_slot[p][:, :], 2 * i + (MOD_START + m + p), p, mod_used)
                            mod_dots.base = None
                    assert steps[0] - start == per, (steps[0] - start, per)
                    steps[0] = start + n * per
                    if l == 0:
                        m += MODS_UP * n
                    u += n
                    residual(PLAN[l, "down", g], G2, s.get("x2_ctx"), g * KB if l == 0 else 0)
                if l == 0:
                    dve.wait_ge(mod_used, m)
                    one_plus(1, SC1, mods_ready)
                    one_plus(1, SC2, mods_ready)
                    dve.wait_ge(mods_ready, 4)
            norm("final", T, 0, None, None)

        @block.tensor
        def _(pe):
            def products(out, cols, w, x_hi, x_lo, first, last):
                wh, wl = w
                for k, (wt, xt) in enumerate(((wh, x_hi), (wh, x_lo), (wl, x_hi))):
                    for a, b in cols:
                        ins = nc.tensor.matmul(out[:, a:b], wt, xt[:, a:b], start=first and k == 0, stop=last and k == 2)
                return ins

            def slab(p, s, uses, order, hi, lo, cols, ready):
                pe.wait_ge(split, 2 * s + 2)
                if uses is not None:
                    pe.wait_ge(drained[p], uses)
                for n, k in enumerate(order):
                    if ready is not None:
                        pe.wait_ge(*ready(n))
                    t = slice(n * P, n * P + P) if order is not Y_ORDER else slice(k * P, k * P + P)
                    ins = products(pair[p], cols, (w_hi[p][:, t], w_lo[p][:, t]), hi[:, k, :], lo[:, k, :],
                                   n == 0, n == len(order) - 1)
                ins.then_inc(done, 1)

            def slabs(first, n, order, hi, lo, cols, ready):
                uses = pair_uses(first)
                if uses == 0:
                    for p in range(2):
                        slab(p, first + p, None, order, hi, lo, cols, ready)
                start = 1 if uses == 0 else 0
                with pe.Fori(start, n) as i:
                    for p in range(2):
                        slab(p, 2 * i + (first + p), i + uses, order, hi, lo, cols, ready)

            def norm(name, ncol, free):
                s = norms[name]
                nch = ncol // P
                for w in free:
                    pe.wait_ge(*w)
                for k in range(KB):
                    pe.wait_ge(s["sq_ready"], k + 1)
                    for c in range(nch):
                        ins = nc.tensor.matmul(aux(2)[:, c:c + 1], sq[k % 2][:, c * P:c * P + P], ones[:, 0:1],
                                               start=k == 0 and c == 0, stop=True, skip_group_check=True)
                    ins.then_inc(s["sq_used"], 1)
                pe.wait_ge(s["rinv_ready"], 1)
                for c in range(nch):
                    ins = nc.tensor.matmul(aux23[:, c * P:c * P + P], rinv[:, c:c + 1].to_broadcast([P, P]),
                                           ident[:, :], start=True, stop=True)
                ins.then_inc(s["rbc_ready"], 1)

            pe.wait_ge(fills, 2)
            pe.wait_ge(consts_loaded, 16 * 7)
            all_k = list(range(KB))
            for l in range(DEPTH):
                s = S[l]
                both, lat = [(0, T), (T, TC)], [(0, T)]
                cols = both if l == 0 else lat
                n1, n2 = norms[f"n1_{l}"], norms[f"n2_{l}"]
                norm(f"n1_{l}", TC, [] if l == 0 else [(norms["n2_0"]["nt_ready"], 2 * KB)])

                def h_ready(sem_, per):
                    return lambda n: (sem_, per * (n + 1))

                slabs(PLAN[l, "kv"], HB, all_k, h_hi, h_lo, both, h_ready(n1["h_ready"], 2))
                n = 0
                pe.wait_ge(*drained_by(PLAN[l, "kv"] + 2 * HB - 1))
                pe.wait_ge(n1["nt_ready"], 2 * KB)
                for src, moved in ((Y, s["v_moved"]), (kT, s["k_moved"])):
                    if src is kT:
                        pe.wait_ge(s["roped"], HB)
                    for c in range(NLC + NCC):
                        if n >= 2:
                            last = n - 2
                            if last < NLC + NCC:
                                pe.wait_ge(s["v_moved"], last + 1)
                            else:
                                pe.wait_ge(s["k_moved"], last - (NLC + NCC) + 1)
                        for j in range(HB):
                            ins = nc.tensor.transpose(aux(2 + n % 2)[:, j * P:j * P + P], src[:, j, c * CH:c * CH + CH],
                                                      ident[:, :])
                        ins.then_inc(s["tr_done"], 1)
                        n += 1
                slabs(PLAN[l, "q"], HB // 2, all_k, h_hi, h_lo, cols, None)
                slabs(PLAN[l, "cch"], FB, all_k, h_hi, h_lo, cols, None)
                slabs(PLAN[l, "cbf"], FB, all_k, h_hi, h_lo, cols, None)

                pe.wait_ge(s["roped"], 2 * HB)
                pe.wait_ge(s["k_moved"], NLC + NCC)
                if l == 0:
                    pe.wait_ge(mods_ready, 2)
                n_state = n_chunk = 0

                def misc_free():
                    if n_state:
                        pe.wait_ge(s["state_ready"], 2 * n_state)
                    if n_chunk:
                        pe.wait_ge(s["o_ready"], n_chunk)

                for item in retention_plan(l):
                    if item[0] == "state":
                        _, d, c, prev, nxt = item
                        misc_free()
                        n_state += 1
                        pe.wait_ge(s["vz_ready"], n_state)
                        for b in range(HB):
                            ins = nc.tensor.matmul(aux(3)[:, b * P:b * P + P], ktok[:, c, b * P:b * P + P],
                                                   vz[:, 2 * b:2 * b + 2, :], start=True, stop=True)
                        ins.then_inc(s["u_done"], 1)
                        continue
                    _, c, col, fwd, bwd = item
                    if n_chunk:
                        pe.wait_ge(s["St_ready"], 2 * n_chunk)
                    for hh in range(2):
                        r = slice(HD * hh, HD * hh + HD)
                        for b in range(HB):
                            ins = nc.tensor.matmul(aux(hh)[:, b * CH:b * CH + CH], kT[r, b, col:col + CH],
                                                   Y[r, b, col:col + CH], start=True, stop=True)
                    ins.then_inc(s["scores_done"], 1)
                    pe.wait_ge(s["qxi_ready"], 2 * (n_chunk + 1))
                    pe.wait_ge(s["state_ready"], 2 * n_state)
                    pe.wait_ge(s["St_ready"], 2 * (n_chunk + 1))
                    if n_chunk:
                        pe.wait_ge(s["osq_ready"], n_chunk)
                    for b in range(HB):
                        out = aux(2)[:, b * CH:b * CH + CH]
                        begun = False
                        for d, st in ((0, fwd), (1, bwd)):
                            if st is not None:
                                nc.tensor.matmul(out, state[st[0]][:, st[1], b, :], qxi[:, d, b, :],
                                                 start=not begun, stop=True, skip_group_check=begun)
                                begun = True
                        for hh in range(2):
                            r = slice(HD * hh, HD * hh + HD)
                            ins = nc.tensor.matmul(aux(2)[r, b * CH:b * CH + CH],
                                                   vtok[:, c, (2 * b + hh) * HD:(2 * b + hh + 1) * HD],
                                                   St[:, hh, b, :], start=False, stop=True, skip_group_check=True)
                    ins.then_inc(s["o_done"], 1)
                    misc_free()
                    pe.wait_ge(s["osq_ready"], n_chunk + 1)
                    for b in range(HB):
                        ins = nc.tensor.matmul(aux(3)[:, 2 * b:2 * b + 2], osq[:, b, :], small[:, 0:2],
                                               start=True, stop=True)
                    ins.then_inc(s["hsum_done"], 1)
                    pe.wait_ge(s["hrinv_ready"], n_chunk + 1)
                    for b in range(HB):
                        for hh in range(2):
                            ins = nc.tensor.matmul(aux(3)[HD * hh:HD * hh + HD, b * CH:b * CH + CH],
                                                   rinv[:, 2 * b + hh:2 * b + hh + 1].to_broadcast([P, HD]),
                                                   ident[:, :], start=True, stop=True)
                    ins.then_inc(s["hbc_done"], 1)
                    n_chunk += 1

                def channels(n):
                    if n >= 2:
                        pe.wait_ge(s["G_split"], n - 1)
                    col = n * CH
                    for b in range(FB):
                        ins = nc.tensor.matmul(aux(n % 2)[:, b * 2 * P:(b + 1) * 2 * P], Y[:, 4 + b, col:col + CH],
                                               chan[:, :], start=True, stop=True)
                    ins.then_inc(s["G_done"], 1)

                pe.wait_ge(s["St_ready"], 2 * n_chunk)
                pe.wait_ge(s["o_ready"], n_chunk)
                nd = dft_slabs(l)
                channels(0)
                for n in range(nd):
                    if n + 1 < nd:
                        channels(n + 1)
                    sl, p = PLAN[l, "dft"] + n, n % 2
                    w = T if n < NLC else C
                    pe.wait_ge(split, 2 * sl + 2)
                    pe.wait_ge(s["G_split"], n + 1)
                    if n == NLC:
                        pe.wait_ge(s["four_ready"], FB)
                    first, last = n in (0, NLC), n in (NLC - 1, nd - 1)
                    for b in range(FB):
                        for t in range(2):
                            g = slice((2 * b + t) * P, (2 * b + t + 1) * P)
                            for k, (G, W) in enumerate(((G_hi, w_hi), (G_lo, w_hi), (G_hi, w_lo))):
                                ins = nc.tensor.matmul(aux(2 + b)[:, 0:w], G[:, n % NLC, g], W[p][:, t * w:(t + 1) * w],
                                                       start=first and t == 0 and k == 0, stop=last and t == 1 and k == 2)
                    ins.then_inc(done, 1)
                slabs(PLAN[l, "g"], HB // 2, all_k, h_hi, h_lo, cols, None)
                slabs(PLAN[l, "out"], KB // 2, Y_ORDER, h_hi, h_lo, cols, h_ready(s["y_split"], 1))
                norm(f"n2_{l}", cols[-1][1], [(s["four_ready"], FB * len(cols))])
                u = 0
                for g, n in enumerate(GROUPS):
                    slabs(PLAN[l, "up", g], n, all_k, h_hi, h_lo, cols, h_ready(n2["h_ready"], len(cols)))
                    slabs(PLAN[l, "down", g], KB // 2, list(range(n)), hid_hi, hid_lo, cols,
                          lambda k: (s["hid_ready"], u + k + 1))
                    u += n
            norm("final", T, [(norms["n2_1"]["nt_ready"], KB)])


def tables():
    i = np.arange(CH)
    diff = i[None, :] - i[:, None]
    parts = []
    rows = T // GRID_W
    n_freq = HD // 4
    freq = ROPE_BASE ** (-np.arange(n_freq, dtype=np.float64) / n_freq)
    row, colm = np.repeat(np.arange(rows), GRID_W), np.tile(np.arange(GRID_W), rows)
    ang = np.concatenate([row[:, None] * freq, colm[:, None] * freq], axis=-1).T
    parts.append(np.tile(np.cos(ang), (4, 1)))
    parts.append(np.tile(np.concatenate([-np.sin(ang), np.sin(ang)]), (2, 1)))
    scale = HD ** -0.5
    parts += [np.maximum(diff, 0), (diff >= 0) * scale, np.maximum(-diff, 0), (diff <= 0) * scale]
    parts += [np.tile(i + 1, (P, 1)), np.tile(CH - i, (P, 1))]
    parts.append(np.eye(P))
    c = np.arange(FG)
    phi = 2 * np.pi * np.outer(c, c) / FG
    for f in (np.cos, np.sin):
        parts.append(np.kron(np.eye(2), f(phi)) / np.sqrt(FG))
    parts.append(np.stack([np.arange(P) < HD, np.arange(P) >= HD, CH - 1 - np.arange(P), np.arange(P)], axis=1))
    return np.concatenate(parts, axis=1).astype(np.float32)


def token_tables(n):
    t = np.arange(n)
    th = 2 * np.pi * (np.outer(t, t) % n) / n
    both = np.concatenate([np.cos(th), -np.sin(th)], axis=1) / np.sqrt(n)
    out = np.zeros((n // P, P, 8 * P), np.float32)
    out[:, :, :2 * n] = both.reshape(n // P, P, 2 * n)
    return out


def tiles(w, row_blocks):
    cols = w.shape[1] // P
    a = w.reshape(row_blocks, P, cols, P).transpose(2, 1, 0, 3).reshape(cols, P, row_blocks * P)
    if row_blocks < 8:
        a = np.concatenate([a, np.zeros((cols, P, (8 - row_blocks) * P), a.dtype)], axis=2)
    return a


def kernel(x, c, ctx, c_ctx, w_mod, b_mod, w_in, ret_decay_logit, mix_conv_w, w_out, ffn_w_up, ffn_conv_w,
           ffn_w_down, final_norm_g):
    import concourse.bacc as bacc
    from concourse.bass_utils import run_bass_kernel_spmd

    slabs = []
    for l in range(DEPTH):
        w = tiles(np.asarray(w_in)[l], KB)
        k0, v0, g0, f0, cb0, cc0, ch0 = 4, 8, 12, 16, 18, 20, 22
        order = [b + j for j in range(HB) for b in (k0, v0)] + list(range(HB))
        order += [b + j for j in range(FB) for b in (cc0, ch0)] + [b + j for j in range(FB) for b in (cb0, f0)]
        slabs.append(w[order])
        slabs.append(token_tables(T))
        if l == 0:
            slabs.append(token_tables(C))
        slabs.append(w[g0:g0 + HB])
        slabs.append(tiles(np.asarray(w_out)[l], KB))
        up = tiles(np.asarray(ffn_w_up)[l], KB)
        b = 0
        for n in GROUPS:
            slabs.append(up[[k for j in range(b, b + n) for k in (j, NHB + j)]])
            slabs.append(tiles(np.asarray(ffn_w_down)[l][b * P:(b + n) * P], n))
            b += n
    slabs = np.concatenate(slabs)
    wm = np.asarray(w_mod)
    mods = np.stack([wm[l, :, (k * KB + b) * P:(k * KB + b + 1) * P].T for l, k, b in MOD_ORDER])
    bm = np.asarray(b_mod)
    bmod = np.stack([bm[l, (k * KB + b) * P:(k * KB + b + 1) * P] for l, k, b in MOD_ORDER], axis=1)
    ffnw = np.asarray(ffn_conv_w).reshape(DEPTH, 3, 2 * NHB, P).transpose(3, 0, 2, 1).reshape(P, -1)
    mixw = np.asarray(mix_conv_w).reshape(DEPTH, 3, FB, P).transpose(3, 0, 2, 1).reshape(P, -1)
    fng = np.asarray(final_norm_g).reshape(KB, P).T
    lg = np.asarray(ret_decay_logit)
    logit = []
    for l in range(DEPTH):
        logit.append(np.broadcast_to(lg[l].reshape(1, 2 * H), (P, 2 * H)))
        logit.append(np.repeat(lg[l].reshape(2 * HB, 2).T, HD, axis=0))
    vecs = np.concatenate([bmod, ffnw, mixw, fng] + logit, axis=1)
    xs = np.concatenate([np.asarray(x)[0], np.asarray(ctx)[0]])
    arrays = {
        "x": xs.T.reshape(KB, P, TC).transpose(1, 0, 2), "c": np.asarray(c).reshape(1, D),
        "c_ctx": np.asarray(c_ctx).reshape(1, D), "slabs": slabs, "mods": mods, "vecs": vecs, "tables": tables(),
    }
    arrays = {f"in_{k}": np.ascontiguousarray(v) for k, v in arrays.items()}
    nc = bacc.Bacc("TRN2", target_bir_lowering=False, num_devices=1)
    io = {k[3:]: nc.dram_tensor(k, v.shape, mybir.dt.from_np(v.dtype), kind="ExternalInput").ap()
          for k, v in arrays.items()}
    io["out"] = nc.dram_tensor("out", (KB, P, T), mybir.dt.float32, kind="ExternalOutput").ap()
    build_program(nc, io)
    r = run_bass_kernel_spmd(nc, [arrays], core_ids=[0])
    out = r.results[0]["out"]
    return np.ascontiguousarray(out.reshape(D, T).T).reshape(1, T, D)
```

```python
import concourse.bass as bass
from concourse import mybir
from concourse.alu_op_type import AluOpType as ALU
import numpy as np

P = 128
T, C = 512, 256
TC = T + C
D = 1024
KB = D // P
DEPTH = 2
H, HD = 8, 64
HB = H * HD // P
CH = 128
NLC, NCC = T // CH, C // CH
FB = 256 // P
FG = 64
HID = 2816
NHB = HID // P
GROUPS = [8, 7, 7]
EPS = 1e-6
GRID_W = 64
ROPE_BASE = 10000.0
SH1, SC1, G1, SH2, SC2, G2 = range(6)
Y_ORDER = [6, 7, 0, 1, 2, 3, 4, 5]


def dft_slabs(layer):
    return NLC + (NCC if layer == 0 else 0)


def stream_plan():
    at, plan = 0, {}
    for l in range(DEPTH):
        for name, n in (("kv", 2 * HB), ("q", HB), ("cch", 2 * FB), ("cbf", 2 * FB), ("g", HB),
                        ("dft", dft_slabs(l)), ("out", KB)):
            plan[l, name] = at
            at += n
        for g, n in enumerate(GROUPS):
            plan[l, "up", g] = at
            at += 2 * n
            plan[l, "down", g] = at
            at += KB
    plan["end"] = at
    return plan


PLAN = stream_plan()


def pair_uses(s):
    return (s - sum(dft_slabs(l) for l in range(DEPTH) if PLAN[l, "dft"] < s)) // 2


MOD_ORDER = ([(0, k, b) for k in (SC1, SH1, G1, SH2, SC2, G2) for b in range(KB)]
             + [(1, k, b) for k in (SC1, SH1, G1, SH2, SC2, G2) for b in range(KB)])
MOD_START = 2 * KB
MODS_KVQ = [3, 3, 4, 4, 2, 0]
MODS_LAST = 2
MODS_OUT = 2
MODS_UP = 2
MOD_KIND = [SC1, SH1, G1, SH2, SC2, G2]


def mod_col(l, kind, b=0):
    return (l * 6 + MOD_KIND.index(kind)) * KB + b


def retention_plan(l):
    c0, c1 = NLC, NLC + 1
    items = [("state", 1, c1, None, ("b", 2)), ("state", 1, c0, ("b", 2), ("b", 3)),
             ("state", 0, c0, None, ("f", 0)), ("state", 0, c1, ("f", 0), ("f", 1))]
    if l == 0:
        items += [("chunk", c0, T, None, ("b", 2)), ("chunk", c1, T + CH, ("f", 0), None)]
    for c in range(NLC - 1, 0, -1):
        items.append(("state", 1, c, ("b", c), ("b", c - 1)))
    for c in range(NLC):
        items.append(("chunk", c, c * CH, ("f", (c + 1) % 2), ("b", c)))
        if c < NLC - 1:
            items.append(("state", 0, c, ("f", (c + 1) % 2), ("f", c % 2)))
    return items


def mixer_plan(l):
    steps = []
    for item in retention_plan(l):
        if item[0] == "state":
            steps.append(item)
        else:
            steps += [(name,) + item[1:] for name in ("scores", "out", "sums", "roots")]
    tiles = [("tile", phase, j, k) for phase, n in (("cch", 2 * FB), ("cbf", 2 * FB), ("g", HB))
             for j in range(n) for k in range(KB)]
    plan, used = [], 0
    for n, step in enumerate(steps):
        upto = len(tiles) * (n + 1) // len(steps)
        plan += tiles[used:upto] + [step]
        used = upto
    return plan


def build_program(nc, io):
    fp32, f32r = mybir.dt.float32, mybir.dt.float32r
    ACT = mybir.ActivationFunctionType

    top = [(nc.sbuf_base + 63) // 64 * 64]

    def at(name, shape, offset, dt=fp32):
        return nc.alloc_sbuf_tensor_at(name, shape, dt, offset=offset)

    def new(name, shape, dt=fp32):
        t = at(name, shape, top[0], dt)
        top[0] += (int(np.prod(shape[1:])) * 4 + 31) // 32 * 32
        return t

    x = new("x", [P, KB, TC])
    h_hi = new("h_hi", [P, KB, TC], f32r)
    h_lo = new("h_lo", [P, KB, TC], f32r)
    raw = [new(f"raw{i}", [P, 8 * P]) for i in range(2)]
    w_hi = [new(f"w_hi{i}", [P, 8 * P], f32r) for i in range(2)]
    w_lo = [new(f"w_lo{i}", [P, 8 * P], f32r) for i in range(2)]
    mask = new("mask", [P, 2, 4, CH])
    xi = new("xi", [P, 2, HB, CH])
    rope_cos = new("rope_cos", [P, T])
    rope_sin = new("rope_sin", [P, T])
    ident = new("ident", [P, P])
    chan = new("chan", [P, 2 * P])
    small = new("small", [P, 4])
    eps = new("eps", [P, 1])
    ones = new("ones", [P, 1])
    gate = new("gate", [P, 1])
    root_probe = new("root_probe", [P, 1])
    n_mod = len(MOD_ORDER)
    modv = new("modv", [P, 2, n_mod])
    mod_acc = new("mod_acc", [P, 2, 2])
    vec_w = {"bmod": n_mod, "ffnw": DEPTH * 2 * NHB * 3, "mixw": DEPTH * FB * 3, "fng": KB, "logit": DEPTH * 24}
    vec_at, n = {}, 0
    for k, v in vec_w.items():
        vec_at[k] = n
        n += v
    vecs = new("vecs", [P, n])
    ld = new("ld", [P, DEPTH * 24])
    ldt = new("ldt", [P, 3, DEPTH * 24])
    zeta = new("zeta", [P, 2, H])
    cdec = new("cdec", [P, 2, HB])
    c_cols = new("c_cols", [P, KB, 2])
    rs = new("rs", [P, 8])
    rinv = new("rinv", [P, 8])
    ct = new("ct", [P, TC])
    work = top[0]
    assert work + 92160 <= nc.sbuf_usable_end, (work + 92160, nc.sbuf_usable_end)

    Y = at("Y", [P, KB, TC], work)
    kT = at("kT", [P, HB, TC], work + 24576)
    ktok = at("ktok", [P, NLC + NCC, 4 * P], work + 36864)
    vtok = at("vtok", [P, NLC + NCC, 4 * P], work + 49152)
    z = at("z", [P, FB, TC], work + 61440)
    state = {"b": at("S_b", [P, NLC, HB, P], work + 67584), "f": at("S_f", [P, 2, HB, P], work + 75776)}
    St = at("St", [P, 2, 4, CH], work + 79872)
    osq = at("osq", [P, HB, CH], work + 86016)
    vz = at("vz", [P, H, HD], work + 83968)
    qxi = at("qxi", [P, 2, HB, CH], work + 88064)
    c_b = at("c_b", [P, 2, D], work + 67584)
    mod_slot = [at(f"mod_slot{i}", [P, D], work + 75776 + 4096 * i) for i in range(2)]
    rot = [at(f"rot{i}", [P, T], work + 83968 + 2048 * i) for i in range(2)]
    eb = at("eb", [P, 2, 4, CH], work + 88064)
    G_hi = at("G_hi", [P, NLC, 4 * P], work + 24576, f32r)
    G_lo = at("G_lo", [P, NLC, 4 * P], work + 32768, f32r)
    sg = [at(f"sg{i}", [P, TC], work + 61440 + 3072 * i) for i in range(2)]
    hid_hi = at("hid_hi", [P, max(GROUPS), TC], work, f32r)
    hid_lo = at("hid_lo", [P, max(GROUPS), TC], work + 24576, f32r)
    tv = at("tv", [P, TC], work + 49152)
    tg = at("tg", [P, TC], work + 52224)
    expo = at("expo", [P, 6, CH], work + 55296)
    sq = [at(f"sq{i}", [P, TC], work + 61440 + 3072 * i) for i in range(2)]
    nt = [at(f"nt{i}", [P, TC], work + 83968 + 3072 * i) for i in range(2)]
    fin = at("fin", [P, KB, T], work)
    sq_sum = at("sq_sum", [P, TC], work + 58368)
    start_slot = [at(f"start_slot{i}", [P, 2 * D], work + (8192 * i if i < 6 else 75776)) for i in range(7)]
    start_rows = at("start_rows", [2, 2 * D], work + 67584)

    pair = [nc.alloc_psum_tensor(f"pair{i}", [P, 1024], fp32) for i in range(2)]
    aux01 = nc.alloc_psum_tensor("aux01", [P, 1024], fp32)
    aux23 = nc.alloc_psum_tensor("aux23", [P, 1024], fp32)

    def aux(i):
        return (aux01 if i < 2 else aux23)[:, (i % 2) * 512:(i % 2) * 512 + 512]

    def by_block(bank):
        return bank.rearrange("p (b i) -> p b i", b=HB)

    sem = nc.alloc_semaphore

    def vec(name, i):
        return vecs[:, vec_at[name] + i:vec_at[name] + i + 1]

    def vec_dyn(name, i):
        return vecs[:, bass.ds(i + vec_at[name], 1)]

    def mod(l, st, kind, b):
        i = mod_col(l, kind, b)
        return modv[:, st, i:i + 1]

    loaded = [sem(f"slab_loaded{i}") for i in range(2)]
    split = sem("slab_split")
    done = sem("slab_done")
    drained = [sem(f"pair_drained{i}") for i in range(2)]
    c_loaded, c_ready = sem("c_loaded"), sem("c_ready")
    x_loaded = [sem(f"x_loaded{i}") for i in range(4)]
    consts_loaded = sem("consts_loaded")
    c_cols_loaded, first_loaded = sem("c_cols_loaded"), sem("first_consts_loaded")
    start_loaded = [sem(f"start_mods_loaded{i}") for i in range(8)]
    start_used, start_rows_ready = sem("start_weights_used"), sem("start_rows_ready")
    start_turned, start_ready = sem("start_mods_turned"), sem("start_mods_ready")
    mod_loaded = [sem(f"mod_loaded{i}") for i in range(2)]
    mod_used, mods_ready = sem("mod_used"), sem("mods_ready")
    fills, gate_done = sem("fills_done"), sem("gate_done")
    out_ready, out_stored = sem("out_ready"), sem("out_stored")
    rot_loaded = [sem(f"rot_loaded{i}") for i in range(2)]
    ld_ready = sem("ld_ready")
    dve_chain = sem("dve_chain")

    S = []
    for l in range(DEPTH):
        names = ["decay_exp", "decay_ready", "roped", "tr_done", "v_moved", "k_moved", "conv_done", "vz_ready",
                 "u_done", "state_ready", "qxi_ready", "scores_done", "St_ready", "o_done", "o_copied", "osq_ready",
                 "hsum_done", "hrs_ready", "hrinv_ready", "hbc_done", "o_ready", "G_done", "G_hi_ready", "G_split",
                 "four_ready", "y_ready", "y_hi", "y_split", "tv_ready", "tg_ready", "silu_ready",
                 "p_ready", "hid_hi_ready", "hid_ready"] + (["x1_ctx", "x2_ctx"] if l == 0 else [])
        S.append({n: sem(f"{n}_{l}") for n in names})
    norms = {n: {k: sem(f"{k}_{n}") for k in ("sq_ready", "sq_added", "sums_done", "rs_ready", "rinv_ready", "rbc_ready",
                                             "nt_ready", "hi_ready", "h_ready")}
             for n in ("n1_0", "n2_0", "n1_1", "n2_1", "final")}

    def layer_cols(l):
        return [(0, 0, T), (1, T, TC)] if l == 0 else [(0, 0, T)]

    def drained_by(s):
        even = s - s % 2
        return drained[s % 2], pair_uses(even) + 1

    block = nc.Block()
    with block:
        @block.sync
        def _(sp):
            def load_slab(s, p):
                sp.dma_start(raw[p][:, :], io["slabs"][s, :, :]).then_inc(loaded[p], 16)

            def load_slabs(first, n):
                with sp.Fori(0, n) as i:
                    for p in range(2):
                        sp.wait_ge(split, 2 * (first + p - 1) + 4 * i)
                        load_slab(first + p + 2 * i, p)

            def load_mods(m, n):
                for j in range(m, m + n):
                    if j >= 2:
                        sp.wait_ge(mod_used, j - 1)
                    sp.dma_start(mod_slot[j % 2][:, :], io["mods"][j, :, :]).then_inc(mod_loaded[j % 2], 16)

            for i in range(KB):
                if i == 7:
                    sp.wait_ge(start_used, 1)
                sp.dma_start(start_slot[i % 7][:, :], io["start_mods"][i, :, :]).then_inc(start_loaded[i], 16)
                if 3 <= i < 7:
                    j = i - 3
                    sp.dma_start(x[:, 2 * j:2 * j + 2, :], io["x"][:, 2 * j:2 * j + 2, :]).then_inc(x_loaded[j], 16)
            load_slab(0, 0)
            load_slab(1, 1)
            tab = io["tables"]
            for dst, src in ((rope_cos[:, :], tab[:, 0:T]), (rope_sin[:, :], tab[:, T:2 * T]),
                             (expo[:, :, :].rearrange("p a b -> p (a b)"), tab[:, 2 * T:2 * T + 6 * CH]),
                             (chan[:, :], tab[:, 1920:2176])):
                sp.dma_start(dst, src).then_inc(consts_loaded, 16)
            s, m = 2, 0
            for n_mods in MODS_KVQ:
                load_slabs(s, 1)
                if s == 2:
                    sp.wait_ge(start_turned, 2)
                    for i, name in enumerate(("c", "c_ctx")):
                        sp.dma_start(c_b[:, i, :], io[name].to_broadcast([P, D])).then_inc(c_loaded, 16)
                load_mods(m, n_mods)
                s, m = s + 2, m + n_mods
            load_slabs(s, (PLAN[0, "out"] + 2 - s) // 2)
            sp.wait_ge(S[0]["o_ready"], NLC + NCC)
            for i in range(KB // 2):
                load_mods(m, MODS_OUT)
                m += MODS_OUT
                load_slabs(PLAN[0, "out"] + 2 + 2 * i, 1)
            for g, n in enumerate(GROUPS):
                s = PLAN[0, "up", g]
                if g == 2:
                    load_slabs(s, 1)
                with sp.Fori(0, n - 1) as i:
                    for p in range(2):
                        sp.wait_ge(split, 2 * (s + 1 + p) + 4 * i)
                        load_slab(s + 2 + p + 2 * i, p)
                        sp.wait_ge(mod_used, m + p - 1 + 2 * i)
                        sp.dma_start(mod_slot[p][:, :], io["mods"][2 * i + (m + p), :, :])\
                            .then_inc(mod_loaded[p], 16)
                m += (n - 1) * MODS_UP
                load_slabs(PLAN[0, "down", g], 1)
                load_mods(m, MODS_UP)
                m += MODS_UP
                if g:
                    load_slabs(PLAN[0, "down", g] + 2, KB // 2 - 1)
                    continue
                for i in range(KB // 2):
                    load_mods(m, MODS_OUT)
                    m += MODS_OUT
                    load_slabs(PLAN[0, "down", g] + 2 + 2 * i, 1)
            s = PLAN[1, "kv"]
            load_slabs(s, 1)
            for _ in range(2):
                s += 2
                load_slabs(s, 1)
                load_mods(m, MODS_LAST)
                m += MODS_LAST
            assert MOD_START + m == n_mod
            load_slabs(s + 2, (PLAN["end"] - s - 2) // 2)
            for k in range(KB):
                sp.wait_ge(out_ready, k + 1)
                sp.dma_start(io["out"][k, :, :], fin[:, k, :]).then_inc(out_stored, 16)
            sp.wait_ge(out_stored, 16 * KB)

        @block.gpsimd
        def _(pool):
            nc.gpsimd.memset(eps[:, :], EPS).then_inc(fills, 1)
            nc.gpsimd.memset(ones[:, :], 1.0).then_inc(fills, 1)

            pool.wait_ge(fills, 2)

            def split_slab(p, n, first):
                pool.wait_ge(loaded[p], 16 * (n + 1))
                if not first:
                    pool.wait_ge(done, 2 * n + (p - 1))
                nc.gpsimd.tensor_tensor(gate[:, 0:1], ones[:, 0:1], ones[:, 0:1], ALU.mult).then_inc(gate_done, 1)
                pool.wait_ge(gate_done, 1)
                nc.gpsimd.tensor_scalar(w_hi[p][:, :], raw[p][:, :], 1.0, 1.0, ALU.mult, ALU.mult).then_inc(split, 1)
                pool.wait_ge(split, 4 * n + (2 * p + 1))
                nc.gpsimd.tensor_tensor(w_lo[p][:, :], raw[p][:, :], w_hi[p][:, :].bitcast(fp32),
                                        ALU.subtract).then_inc(split, 1)
            for p in range(2):
                split_slab(p, 0, True)
            with pool.Fori(1, PLAN["end"] // 2) as i:
                for p in range(2):
                    split_slab(p, i, False)

        @block.scalar
        def _(act):
            tab = io["tables"]
            act.dma_start(c_cols[:, :, :], io["c_cols"]).then_inc(c_cols_loaded, 16)
            for dst, src in ((vecs[:, :], io["vecs"]), (ident[:, :], tab[:, 1792:1920]), (small[:, :], tab[:, 2176:2180])):
                act.dma_start(dst, src).then_inc(first_loaded, 16)
            act.wait_ge(c_cols_loaded, 16)
            nc.scalar.activation(c_cols[:, :, :], c_cols[:, :, :], ACT.Silu).then_inc(c_ready, 1)
            act.wait_ge(fills, 2)
            act.wait_ge(first_loaded, 16 * 3)
            act.wait_ge(ld_ready, 1)
            nc.scalar.activation(ldt[:, 0, :], ldt[:, 1, :], ACT.Exp, scale=-1.0).then_inc(ld_ready, 1)
            act.wait_ge(ld_ready, 3)

            def decays(l):
                s, o = S[l], l * 24
                if l:
                    act.wait_ge(S[0]["hid_ready"], NHB)
                act.wait_ge(consts_loaded, 16 * (4 + l))
                for d, dst in ((0, mask), (1, eb)):
                    for hh in range(H):
                        nc.scalar.activation(dst[:, hh % 2, hh // 2, :], expo[:, 2 * d, :], ACT.Exp,
                                             scale=ld[:, o + 8 * d + hh:o + 8 * d + hh + 1]).then_inc(s["decay_exp"], 1)
                for d in range(2):
                    for b in range(HB):
                        q = o + 16 + 4 * d + b
                        nc.scalar.activation(xi[:, d, b, :], expo[:, 4 + d, :], ACT.Exp, scale=ld[:, q:q + 1])\
                            .then_inc(s["decay_exp"], 1)
                    nc.scalar.activation(zeta[:, d, :], ld[:, o + 8 * d:o + 8 * d + 8], ACT.Exp,
                                         scale=small[:, 2 + d:3 + d]).then_inc(s["decay_exp"], 1)
                nc.scalar.activation(cdec[:, :, :].rearrange("p a b -> p (a b)"), ld[:, o + 16:o + 24], ACT.Exp,
                                     scale=float(CH)).then_inc(s["decay_exp"], 1)

            def norm(name, ncol, l, sh, x_ready):
                s = norms[name]
                for k in range(KB):
                    x_ready(k)
                    if k == 0:
                        nc.scalar.activation(root_probe[:, :], eps[:, :], ACT.Sqrt)
                    if k >= 3:
                        act.wait_ge(s["sq_added"], k - 2)
                    nc.scalar.activation((sq[k % 2] if k else sq_sum)[:, 0:ncol], x[:, k, 0:ncol], ACT.Square)\
                        .then_inc(s["sq_ready"], 1)
                act.wait_ge(s["sums_done"], 1)
                nc.scalar.activation(rs[:, 0:ncol // P], aux(2)[:, 0:ncol // P], ACT.Sqrt, bias=eps[:, 0:1],
                                     scale=1.0 / D).then_inc(s["rs_ready"], 1)
                if sh is None:
                    return
                if name == "n1_0":
                    act.wait_ge(start_used, KB)
                    nc.scalar.activation(start_rows[:, 0:D], pair[0][0:2, :], ACT.Copy).then_inc(start_rows_ready, 1)
                cols = [(0, 0, T)] + ([(1, T, TC)] if ncol == TC else [])
                for k in range(KB):
                    for st, a, b in cols:
                        act.wait_ge(s["nt_ready"], len(cols) * k + st + 1)
                        nc.scalar.activation(h_hi[:, k, a:b], nt[k % 2][:, a:b], ACT.Identity,
                                             bias=mod(l, st, sh, k)).then_inc(s["hi_ready"], 1)

            def x_after(first_slab, ctx):
                def ready(k):
                    act.wait_ge(*drained_by(first_slab + k))
                    if ctx is not None:
                        act.wait_ge(ctx[0], ctx[1] + k + 1)
                return ready

            for l in range(DEPTH):
                s = S[l]
                cols = layer_cols(l)
                nlat = cols[-1][2]
                if l == 0:
                    norm("n1_0", TC, 0, SH1, lambda k: act.wait_ge(x_loaded[k // 2], 16))
                else:
                    norm("n1_1", TC, 1, SH1, x_after(PLAN[0, "down", 2], (S[0]["x2_ctx"], 2 * KB)))

                def copy_out(slab, dst, ncol):
                    p = slab % 2
                    act.wait_ge(done, slab + 1)
                    nc.scalar.activation(dst, pair[p][:, 0:ncol], ACT.Copy).then_inc(drained[p], 1)

                def swap(src, slab, unit):
                    p = unit % 2
                    act.wait_ge(*drained_by(slab))
                    if unit >= 2:
                        act.wait_ge(s["roped"], unit - 1)
                    for g in range(4):
                        a, b = 32 * g, 32 * (g ^ 1)
                        act.dma_start(rot[p][a:a + 32, :], src[b:b + 32]).then_inc(rot_loaded[p], 16)

                kv, q0 = PLAN[l, "kv"], PLAN[l, "q"]
                for j in range(HB):
                    copy_out(kv + 2 * j, kT[:, j, :], TC)
                    swap(kT[:, j, 0:T], kv + 2 * j, j)
                    copy_out(kv + 2 * j + 1, Y[:, j, :], TC)
                    if j == 0:
                        if l == 0:
                            act.wait_ge(c_loaded, 32)
                            nc.scalar.activation(c_b[:, :, :], c_b[:, :, :], ACT.Silu).then_inc(c_ready, 1)
                        decays(l)
                for c in range(NLC + NCC):
                    act.wait_ge(s["tr_done"], c + 1)
                    nc.scalar.activation(vtok[:, c, :], aux(2 + c % 2), ACT.Copy).then_inc(s["v_moved"], 1)
                for j in range(HB):
                    if j == HB - 1:
                        for c in range(NLC + NCC):
                            u = NLC + NCC + c
                            act.wait_ge(s["tr_done"], u + 1)
                            nc.scalar.activation(ktok[:, c, :], aux(2 + u % 2), ACT.Copy).then_inc(s["k_moved"], 1)
                    copy_out(q0 + j, Y[:, j, 0:nlat], nlat)
                    swap(Y[:, j, 0:T], q0 + j, HB + j)

                def gate(j):
                    slab, p = PLAN[l, "g"] + j, j % 2
                    act.wait_ge(done, slab + 1)
                    if j >= 2:
                        act.wait_ge(s["y_ready"], j - 1)
                    nc.scalar.activation(sg[p][:, 0:nlat], pair[p][:, 0:nlat], ACT.Silu).then_inc(drained[p], 1)

                n = 0
                for step in mixer_plan(l):
                    if step[0] == "tile":
                        _, phase, j, k = step
                        if k < KB - 1:
                            continue
                        slab = PLAN[l, phase] + j
                        if phase == "cch" and j % 2 == 0:
                            copy_out(slab, z[:, j // 2, 0:nlat], nlat)
                        elif phase == "cbf":
                            copy_out(slab, Y[:, (4 if j % 2 else 6) + j // 2, 0:nlat], nlat)
                        elif phase == "g" and j < 2:
                            act.wait_ge(s["conv_done"], FB)
                            gate(j)
                    elif step[0] == "out":
                        col = step[2]
                        act.wait_ge(s["o_done"], n + 1)
                        nc.scalar.activation(Y[:, 0:HB, col:col + CH], by_block(aux(2)), ACT.Copy)\
                            .then_inc(s["o_copied"], 1)
                        nc.scalar.activation(osq[:, :, :], by_block(aux(2)), ACT.Square).then_inc(s["osq_ready"], 1)
                    elif step[0] == "sums":
                        act.wait_ge(s["hsum_done"], n + 1)
                        nc.scalar.activation(rs[:, 0:H], aux(3)[:, 0:H], ACT.Sqrt, bias=eps[:, 0:1], scale=1.0 / HD)\
                            .then_inc(s["hrs_ready"], 1)
                        n += 1
                if l == 0:
                    act.wait_ge(s["o_ready"], n)
                    for i, name in enumerate(("c", "c_ctx")):
                        act.dma_start(c_b[:, i, :], io[name].to_broadcast([P, D])).then_inc(c_loaded, 16)
                    act.dma_start(expo[:, :, :].rearrange("p a b -> p (a b)"), tab[:, 2 * T:2 * T + 6 * CH])\
                        .then_inc(consts_loaded, 16)

                def output_hi(k):
                    if k < HB:
                        act.wait_ge(s["y_ready"], k + 1)
                    elif k == 4:
                        act.wait_ge(s["four_ready"], FB * (2 if l == 0 else 1))
                    elif k == 6:
                        act.wait_ge(s["conv_done"], FB)
                        act.wait_ge(done, PLAN[l, "g"] + HB)
                    nc.scalar.activation(h_hi[:, k, 0:nlat], Y[:, k, 0:nlat], ACT.Copy).then_inc(s["y_hi"], 1)

                for n in range(dft_slabs(l)):
                    act.wait_ge(s["G_done"], n + 1)
                    if n >= NLC:
                        act.wait_ge(done, PLAN[l, "dft"] + n - NLC + 1)
                    nc.scalar.activation(G_hi[:, n % NLC, :], aux(n % 2), ACT.Copy).then_inc(s["G_hi_ready"], 1)
                    if n < 2:
                        gate(2 + n)
                    elif n >= dft_slabs(l) - 2:
                        output_hi(Y_ORDER[n - dft_slabs(l) + 2])
                for k in Y_ORDER[2:]:
                    output_hi(k)
                if l == 0:
                    act.wait_ge(c_loaded, 64)
                    nc.scalar.activation(c_b[:, :, :], c_b[:, :, :], ACT.Silu).then_inc(c_ready, 1)
                norm(f"n2_{l}", nlat, l, SH2, x_after(PLAN[l, "out"], (s["x1_ctx"], 0) if l == 0 else None))
                u = 0
                for g, n in enumerate(GROUPS):
                    s0 = PLAN[l, "up", g]

                    def hidden(i, first):
                        act.wait_ge(done, s0 + 1 + 2 * i)
                        if not first:
                            act.wait_ge(s["hid_ready"], u + i)
                        w = (l * 2 * NHB + u) * 3 + 1 + 3 * i
                        nc.scalar.activation(tv[:, 0:nlat], pair[0][:, 0:nlat], ACT.Copy, scale=vec_dyn("ffnw", w))\
                            .then_inc(s["tv_ready"], 1)
                        act.wait_ge(done, s0 + 2 + 2 * i)
                        nc.scalar.activation(tg[:, 0:nlat], pair[1][:, 0:nlat], ACT.Copy,
                                             scale=vec_dyn("ffnw", w + 3 * NHB)).then_inc(s["tg_ready"], 1)
                        act.wait_ge(drained[1], pair_uses(s0) + 1 + i)
                        nc.scalar.activation(tg[:, 0:nlat], tg[:, 0:nlat], ACT.Silu).then_inc(s["silu_ready"], 1)
                        act.wait_ge(s["p_ready"], u + 1 + i)
                        nc.scalar.activation(hid_hi[:, i, 0:nlat], tv[:, 0:nlat], ACT.Copy)\
                            .then_inc(s["hid_hi_ready"], 1)
                    hidden(0, u == 0)
                    with act.Fori(1, n) as i:
                        hidden(i, False)
                    u += n
            norm("final", T, 0, None, x_after(PLAN[1, "down", 2], None))

        @block.vector
        def _(dve):
            steps = [0]

            def chain(ins, base=None):
                steps[0] += 1
                ins.then_inc(dve_chain, 1)
                dve.wait_ge(dve_chain, steps[0] if base is None else base + steps[0])

            def mod_dots(slab, col, acc, used):
                for st in range(2):
                    chain(nc.vector.tensor_tensor_reduce(out=aux01[:, :], in0=slab, in1=c_b[:, st, :], scale=1.0,
                                                         scalar=0.0, op0=ALU.mult, op1=ALU.add,
                                                         accum_out=mod_acc[:, acc, st:st + 1]), mod_dots.base)
                nc.vector.tensor_tensor(modv[:, :, bass.ds(col, 1)], mod_acc[:, acc, :].unsqueeze(2),
                                        vec_dyn("bmod", col).unsqueeze(1).to_broadcast([P, 2, 1]), ALU.add)\
                    .then_inc(used, 1)
            mod_dots.base = None

            def ring_mods(m, n):
                for j in range(m, m + n):
                    dve.wait_ge(mod_loaded[j % 2], 16 * (j // 2 + 1))
                    mod_dots(mod_slot[j % 2][:, :], MOD_START + j, j % 2, mod_used)

            def one_plus(l, kind, ready):
                c = mod_col(l, kind)
                nc.vector.tensor_scalar(modv[:, :, c:c + KB], modv[:, :, c:c + KB], 1.0, None, ALU.add).then_inc(ready, 1)

            dve.wait_ge(fills, 2)
            dve.wait_ge(first_loaded, 16 * 3)
            lg = vecs[:, vec_at["logit"]:vec_at["logit"] + DEPTH * 24]
            ya, yb, yc = ldt[:, 0, :], ldt[:, 1, :], ldt[:, 2, :]
            chain(nc.vector.tensor_scalar(yb, lg, -1.0, None, ALU.mult))
            nc.vector.tensor_tensor(yb, yb, lg, ALU.max).then_inc(ld_ready, 1)
            dve.wait_ge(ld_ready, 2)
            chain(nc.vector.tensor_scalar(yb, ya, 2.0, None, ALU.add))
            chain(nc.vector.reciprocal(yb, yb))
            chain(nc.vector.tensor_tensor(ya, ya, yb, ALU.mult))
            chain(nc.vector.tensor_tensor(yb, ya, ya, ALU.mult))
            chain(nc.vector.tensor_scalar(yc, yb, 1.0 / 17, None, ALU.mult))
            for k in range(15, 1, -2):
                chain(nc.vector.scalar_tensor_tensor(yc, yc, 1.0 / k, yb, ALU.add, ALU.mult))
            chain(nc.vector.scalar_tensor_tensor(yc, yc, 1.0, ya, ALU.add, ALU.mult))
            chain(nc.vector.tensor_scalar(yb, lg, 0.0, None, ALU.min))
            nc.vector.scalar_tensor_tensor(ld[:, :], yc, -2.0, yb, ALU.mult, ALU.add).then_inc(ld_ready, 1)

            def decays(l):
                s = S[l]
                dve.wait_ge(s["decay_exp"], 27)
                for p in range(2):
                    chain(nc.vector.tensor_tensor(mask[:, p, :, :], mask[:, p, :, :],
                                                  expo[:, 1:2, :].to_broadcast([P, 4, CH]), ALU.mult))
                    chain(nc.vector.tensor_tensor(eb[:, p, :, :], eb[:, p, :, :],
                                                  expo[:, 3:4, :].to_broadcast([P, 4, CH]), ALU.mult))
                    chain(nc.vector.tensor_tensor(mask[:, p, :, :], mask[:, p, :, :], eb[:, p, :, :], ALU.add))
                chain(nc.vector.tensor_scalar(zeta[:, :, :], zeta[:, :, :], HD ** -0.5, None, ALU.mult))

            def add_square(name, ncol, p, k):
                s = norms[name]
                dve.wait_ge(s["sq_ready"], k + 1)
                if type(k) is not int or k > 1:
                    dve.wait_ge(s["sq_added"], k - 1)
                nc.vector.tensor_tensor(sq_sum[:, 0:ncol], sq_sum[:, 0:ncol], sq[p][:, 0:ncol], ALU.add)\
                    .then_inc(s["sq_added"], 1)

            def norm(name, ncol, l, sc, sh):
                s = norms[name]
                cols = [(0, 0, T)] + ([(1, T, TC)] if ncol == TC else [])
                if name == "n1_0":
                    for k in range(1, KB - 1):
                        add_square(name, ncol, k % 2, k)
                dve.wait_ge(s["rs_ready"], 1)
                nc.vector.reciprocal(rinv[:, 0:ncol // P], rs[:, 0:ncol // P]).then_inc(s["rinv_ready"], 1)
                dve.wait_ge(s["rbc_ready"], 1)

                if name == "n1_0":
                    dve.wait_ge(start_used, KB)
                    nc.vector.tensor_copy(start_rows[:, D:2 * D], pair[1][0:2, :]).then_inc(start_rows_ready, 1)


                def first_mods(group, b0, n):
                    dve.wait_ge(start_turned, group + 1)
                    for i, one in ((b0, 1.0), (KB + b0, 0.0)):
                        nc.vector.scalar_tensor_tensor(
                            modv[:, :, i:i + n], aux(1 - group)[:, 2 * i:2 * i + 2 * n].rearrange("p (b s) -> p s b", s=2),
                            one, vecs[:, vec_at["bmod"] + i:vec_at["bmod"] + i + n].unsqueeze(1).to_broadcast([P, 2, n]),
                            ALU.add, ALU.add).then_inc(start_ready, 1)
                    dve.wait_ge(start_ready, 2 * group + 2)

                def scale(k):
                    if name == "n1_0" and k < 2:
                        first_mods(k, k, 1 if k == 0 else KB - 1)
                    for st, a, b in cols:
                        if k == 0:
                            dve.wait_ge(s["rbc_ready"], st + 1)
                        nc.vector.scalar_tensor_tensor(nt[k % 2][:, a:b], aux23[:, a:b], mod(l, st, sc, k),
                                                       x[:, k, a:b], ALU.mult, ALU.mult).then_inc(s["nt_ready"], 1)

                if sc is None:
                    for k in range(KB):
                        nc.vector.scalar_tensor_tensor(fin[:, k, :], aux23[:, 0:T], vec("fng", k), x[:, k, 0:T],
                                                       ALU.mult, ALU.mult).then_inc(out_ready, 1)
                    return
                scale(0)
                for k in range(KB):
                    if k + 1 < KB:
                        if k:
                            dve.wait_ge(s["h_ready"], len(cols) * k)
                        scale(k + 1)
                    for st, a, b in cols:
                        dve.wait_ge(s["hi_ready"], len(cols) * k + st + 1)
                        nc.vector.scalar_tensor_tensor(h_lo[:, k, a:b], nt[k % 2][:, a:b], mod(l, st, sh, k),
                                                       h_hi[:, k, a:b].bitcast(fp32), ALU.add, ALU.subtract)\
                            .then_inc(s["h_ready"], 1)

            def clear_states():
                for t in state.values():
                    chain(nc.vector.memset(t[:, :, :, :], 0.0))

            m = 0
            for l in range(DEPTH):
                s = S[l]
                cols = layer_cols(l)
                nlat = cols[-1][2]
                norm(f"n1_{l}", TC, l, SC1, SH1)

                def rope(buf, unit):
                    p = unit % 2
                    dve.wait_ge(rot_loaded[p], 64 * (l * HB + unit // 2 + 1))
                    chain(nc.vector.tensor_tensor(rot[p][:, :], rot[p][:, :], rope_sin[:, :], ALU.mult))
                    chain(nc.vector.tensor_tensor(buf, buf, rope_cos[:, :], ALU.mult))
                    nc.vector.tensor_tensor(buf, buf, rot[p][:, :], ALU.add).then_inc(s["roped"], 1)

                for j in range(HB):
                    if j == 0:
                        dve.wait_ge(consts_loaded, 16 * 4)
                    rope(kT[:, j, 0:T], j)
                    if l == 0:
                        if j == 0:
                            dve.wait_ge(c_ready, 2)
                        ring_mods(m, MODS_KVQ[j])
                        m += MODS_KVQ[j]
                    elif j < 2:
                        ring_mods(m, MODS_LAST)
                        m += MODS_LAST
                    if j == 0:
                        decays(l)
                    if l and j == 1:
                        dve.wait_ge(mod_used, m)
                        clear_states()
                for j in range(HB):
                    if l == 0 and j % 2:
                        ring_mods(m, MODS_KVQ[HB + j // 2])
                        m += MODS_KVQ[HB + j // 2]
                    if j < HB - 1:
                        rope(Y[:, j, 0:T], HB + j)

                def convolution(b):
                    w = [vec("mixw", (l * FB + b) * 3 + t) for t in range(3)]
                    dve.wait_ge(*drained_by(PLAN[l, "cch"] + 2 * b + 1))
                    if b:
                        dve.wait_ge(s["conv_done"], b)
                    chain(nc.vector.tensor_scalar(ct[:, 0:nlat], z[:, b, 0:nlat], w[1], None, ALU.mult))
                    for _, a0, a1 in cols:
                        chain(nc.vector.scalar_tensor_tensor(ct[:, a0 + 1:a1], z[:, b, a0:a1 - 1], w[0],
                                                             ct[:, a0 + 1:a1], ALU.mult, ALU.add))
                        chain(nc.vector.scalar_tensor_tensor(ct[:, a0:a1 - 1], z[:, b, a0 + 1:a1], w[2],
                                                             ct[:, a0:a1 - 1], ALU.mult, ALU.add))
                    dve.wait_ge(*drained_by(PLAN[l, "cbf"] + 2 * b))
                    nc.vector.tensor_tensor(Y[:, 6 + b, 0:nlat], Y[:, 6 + b, 0:nlat], ct[:, 0:nlat], ALU.mult)\
                        .then_inc(s["conv_done"], 1)

                if l == 0:
                    dve.wait_ge(mod_used, m)

                if l == 0:
                    clear_states()
                dve.wait_ge(s["roped"], 2 * HB - 1)
                n_state = n_chunk = 0
                conv_due = []
                for item in mixer_plan(l):
                    if item[0] == "tile":
                        _, phase, j, k = item
                        if k == KB - 1 and phase == "cch" and j % 2:
                            slab, b = PLAN[l, "cch"] + j, j // 2
                            dve.wait_ge(*drained_by(slab - 1))
                            dve.wait_ge(done, slab + 1)
                            nc.vector.tensor_tensor(z[:, b, 0:nlat], pair[1][:, 0:nlat], z[:, b, 0:nlat], ALU.mult)\
                                .then_inc(drained[1], 1)
                        if k == KB - 1 and phase == "cbf" and j % 2 == 0:
                            conv_due.append(j // 2)
                        if k == KB - 1 and phase == "g" and j == 0:
                            while conv_due:
                                convolution(conv_due.pop(0))
                        continue
                    if item[0] == "state":
                        _, d, c, prev, nxt = item
                        nc.vector.tensor_tensor(vz[:, :, :], vtok[:, c, :].rearrange("p (h e) -> p h e", h=H),
                                                zeta[:, d, :].unsqueeze(2).to_broadcast([P, H, HD]), ALU.mult)\
                            .then_inc(s["vz_ready"], 1)
                        n_state += 1
                        dve.wait_ge(s["u_done"], n_state)
                        to = state[nxt[0]][:, nxt[1], :, :]
                        for hh in range(2):
                            r = slice(HD * hh, HD * hh + HD)
                            U = by_block(aux(3))[r, :, r]
                            if prev is None:
                                nc.vector.tensor_copy(to[r, :, r], U).then_inc(s["state_ready"], 1)
                            else:
                                chain(nc.vector.tensor_tensor(to[r, :, r], state[prev[0]][r, prev[1], :, r],
                                                              cdec[r, d, :].unsqueeze(2).to_broadcast([HD, HB, HD]),
                                                              ALU.mult))
                                nc.vector.tensor_tensor(to[r, :, r], U, to[r, :, r], ALU.add)\
                                    .then_inc(s["state_ready"], 1)
                        dve.wait_ge(s["state_ready"], 2 * n_state)
                        continue
                    name, c, col, fwd, bwd = item
                    q = Y[:, 0:HB, col:col + CH]
                    if name == "out" and conv_due:
                        convolution(conv_due.pop(0))
                    if name == "scores":
                        if n_chunk == 0:
                            rope(Y[:, HB - 1, 0:T], 2 * HB - 1)
                            dve.wait_ge(s["roped"], 2 * HB)
                        for d, st in ((0, fwd), (1, bwd)):
                            nc.vector.tensor_tensor(qxi[:, d, :, :], q, xi[:, d, :, :], ALU.mult)\
                                .then_inc(s["qxi_ready"], 1)
                        dve.wait_ge(s["scores_done"], n_chunk + 1)
                        for p in range(2):
                            nc.vector.tensor_tensor(St[:, p, :, :], by_block(aux(p)), mask[:, p, :, :], ALU.mult)\
                                .then_inc(s["St_ready"], 1)
                    elif name == "sums":
                        dve.wait_ge(s["hrs_ready"], n_chunk + 1)
                        nc.vector.reciprocal(rinv[:, 0:H], rs[:, 0:H]).then_inc(s["hrinv_ready"], 1)
                    elif name == "roots":
                        dve.wait_ge(s["hbc_done"], n_chunk + 1)
                        dve.wait_ge(s["o_copied"], n_chunk + 1)
                        nc.vector.tensor_tensor(q, by_block(aux(3)), q, ALU.mult).then_inc(s["o_ready"], 1)
                        n_chunk += 1
                dve.wait_ge(s["o_ready"], n_chunk)

                def gated(j):
                    dve.wait_ge(*drained_by(PLAN[l, "g"] + j))
                    nc.vector.tensor_tensor(Y[:, j, 0:nlat], Y[:, j, 0:nlat], sg[j % 2][:, 0:nlat], ALU.mult)\
                        .then_inc(s["y_ready"], 1)

                def output_lo(n):
                    k = Y_ORDER[n]
                    dve.wait_ge(s["y_hi"], n + 1)
                    nc.vector.tensor_tensor(h_lo[:, k, 0:nlat], Y[:, k, 0:nlat], h_hi[:, k, 0:nlat].bitcast(fp32),
                                            ALU.subtract).then_inc(s["y_split"], 1)

                gated(0)
                gated(1)
                for n in range(dft_slabs(l)):
                    dve.wait_ge(s["G_hi_ready"], n + 1)
                    nc.vector.tensor_tensor(G_lo[:, n % NLC, :], aux(n % 2), G_hi[:, n % NLC, :].bitcast(fp32),
                                            ALU.subtract).then_inc(s["G_split"], 1)
                    if n < 2:
                        gated(2 + n)
                    elif n >= dft_slabs(l) - 2:
                        output_lo(n - dft_slabs(l) + 2)
                    if n == dft_slabs(l) - 1:
                        parts = [(NLC, 0, T)] + ([(NLC + NCC, T, TC)] if l == 0 else [])
                        for count, a0, a1 in parts:
                            dve.wait_ge(done, PLAN[l, "dft"] + count)
                            for b in range(FB):
                                src = aux(2 + b)[:, 0:T] if a0 == 0 else aux(0)[:, b * C:b * C + C]
                                nc.vector.tensor_copy(Y[:, 4 + b, a0:a1], src).then_inc(s["four_ready"], 1)
                for n in range(2, KB):
                    output_lo(n)

                def residual(first, kind, ctx_ready, ctx_before=0, mods=None, name=None):
                    start, per = steps[0], 0 if mods is None else 4
                    c0 = mod_col(l, kind)
                    for p in range(2):
                        dve.wait_ge(drained[p], pair_uses(first))
                    if ctx_before:
                        dve.wait_ge(ctx_ready, ctx_before)

                    def two_blocks(i):
                        for p in range(2):
                            if mods is not None:
                                mod_dots.base = per * i
                                dve.wait_ge(mod_loaded[p], 16 * (mods // 2 + 1) + 16 * i)
                                mod_dots(mod_slot[p][:, :], 2 * i + (MOD_START + mods + p), p, mod_used)
                                mod_dots.base = None
                            if name and type(i) is not int:
                                add_square(name, nlat, 1 - p, 2 * i + (p - 1))
                            dve.wait_ge(done, first + p + 1 + 2 * i)
                            for st, a0, a1 in reversed(cols):
                                nc.vector.scalar_tensor_tensor(
                                    x[:, 2 * i + p, a0:a1], pair[p][:, a0:a1], modv[:, st, bass.ds(2 * i + (c0 + p), 1)],
                                    x[:, 2 * i + p, a0:a1], ALU.mult, ALU.add)\
                                    .then_inc(drained[p] if st == 0 else ctx_ready, 1)

                    if name:
                        two_blocks(0)
                        steps[0] = start
                    with dve.Fori(1 if name else 0, KB // 2) as i:
                        two_blocks(i)
                    steps[0] = start + per * (KB // 2)

                if l == 0:
                    dve.wait_ge(c_ready, 3)
                residual(PLAN[l, "out"], G1, s.get("x1_ctx"), 0, m if l == 0 else None, f"n2_{l}")
                if l == 0:
                    m += KB
                    dve.wait_ge(mod_used, m)
                    one_plus(0, SC2, mods_ready)
                    dve.wait_ge(mods_ready, 1)
                norm(f"n2_{l}", nlat, l, SC2, SH2)
                u = 0
                for g, n in enumerate(GROUPS):
                    s0 = PLAN[l, "up", g]
                    per = 2 * (2 * len(cols) - 1) + (2 * MODS_UP if l == 0 else 0)
                    start = steps[0]
                    with dve.Fori(0, n) as i:
                        base = i * per

                        def outer_taps(t, p, w):
                            ops = []
                            for _, a0, a1 in cols:
                                ops += [(t[:, a0 + 1:a1], pair[p][:, a0:a1 - 1], 0),
                                        (t[:, a0:a1 - 1], pair[p][:, a0 + 1:a1], 2)]
                            for k, (dst, src, tap) in enumerate(ops):
                                ins = nc.vector.scalar_tensor_tensor(dst, src, vec_dyn("ffnw", w + tap), dst,
                                                                     ALU.mult, ALU.add)
                                if k < len(ops) - 1:
                                    chain(ins, base)
                                else:
                                    ins.then_inc(drained[p], 1)

                        w = (l * 2 * NHB + u) * 3 + 3 * i

                        def block_mods(p):
                            if l == 0:
                                mod_dots.base = base
                                dve.wait_ge(mod_loaded[p], 16 * (m // 2 + 1) + 16 * i)
                                mod_dots(mod_slot[p][:, :], 2 * i + (MOD_START + m + p), p, mod_used)
                                mod_dots.base = None

                        dve.wait_ge(s["tv_ready"], u + 1 + i)
                        outer_taps(tv, 0, w)
                        block_mods(0)
                        dve.wait_ge(s["tg_ready"], u + 1 + i)
                        outer_taps(tg, 1, w + 3 * NHB)
                        block_mods(1)
                        dve.wait_ge(s["silu_ready"], u + 1 + i)
                        dve.wait_ge(drained[0], pair_uses(s0) + 1 + i)
                        nc.vector.tensor_tensor(tv[:, 0:nlat], tv[:, 0:nlat], tg[:, 0:nlat], ALU.mult)\
                            .then_inc(s["p_ready"], 1)
                        dve.wait_ge(s["hid_hi_ready"], u + 1 + i)
                        nc.vector.tensor_tensor(hid_lo[:, i, 0:nlat], tv[:, 0:nlat],
                                                hid_hi[:, i, 0:nlat].bitcast(fp32), ALU.subtract)\
                            .then_inc(s["hid_ready"], 1)
                    assert steps[0] - start == per, (steps[0] - start, per)
                    steps[0] = start + n * per
                    if l == 0:
                        m += MODS_UP * n
                    u += n
                    more = l == 0 and g == 0
                    residual(PLAN[l, "down", g], G2, s.get("x2_ctx"), g * KB if l == 0 else 0, m if more else None,
                             None if g < len(GROUPS) - 1 else "final" if l else "n1_1")
                    if more:
                        m += KB
                if l == 0:
                    dve.wait_ge(mod_used, m)
                    one_plus(1, SC1, mods_ready)
                    one_plus(1, SC2, mods_ready)
                    dve.wait_ge(mods_ready, 3)
            norm("final", T, 0, None, None)

        @block.tensor
        def _(pe):
            def products(out, cols, w, x_hi, x_lo, first, last, lo_ready):
                wh, wl = w
                for k, (wt, xt) in enumerate(((wh, x_hi), (wl, x_hi), (wh, x_lo))):
                    if k == 2 and lo_ready is not None:
                        pe.wait_ge(*lo_ready)
                    for a, b in cols:
                        ins = nc.tensor.matmul(out[:, a:b], wt, xt[:, a:b], start=first and k == 0, stop=last and k == 2)
                return ins

            def begin(p, s, uses):
                pe.wait_ge(split, 2 * s + 2)
                if uses is not None:
                    pe.wait_ge(drained[p], uses)

            def tile(p, n, order, hi, lo, cols, ready):
                k = order[n]
                hi_ready, lo_ready = ready(n) if ready is not None else (None, None)
                if hi_ready is not None:
                    pe.wait_ge(*hi_ready)
                t = slice(n * P, n * P + P) if order is not Y_ORDER else slice(k * P, k * P + P)
                ins = products(pair[p], cols, (w_hi[p][:, t], w_lo[p][:, t]), hi[:, k, :], lo[:, k, :],
                               n == 0, n == len(order) - 1, lo_ready)
                if n == len(order) - 1:
                    ins.then_inc(done, 1)

            def slab(p, s, uses, order, *rest):
                begin(p, s, uses)
                for n in range(len(order)):
                    tile(p, n, order, *rest)

            def in_turns(n, lag):
                return [(p, k - lag * p) for k in range(n + lag) for p in range(2) if 0 <= k - lag * p < n]

            def last_late(n, others):
                return ([(0, k) for k in range(n - 1)] + [(1, k) for k in range(others)] + [(0, n - 1)]
                        + [(1, k) for k in range(others, n)])

            def first_pair(first, order, hi, lo, cols, ready, turns):
                uses = pair_uses(first) or None
                for p, k in turns:
                    if k == 0:
                        begin(p, first + p, uses)
                    tile(p, k, order, hi, lo, cols, ready)

            def start_mods(k):
                pe.wait_ge(start_loaded[k], 16)
                for j in range(4):
                    ins = nc.tensor.matmul(pair[j // 2][0:2, j % 2 * 512:j % 2 * 512 + 512], c_cols[:, k, :],
                                           start_slot[k % 7][:, j * 512:j * 512 + 512], start=k == 0, stop=k == KB - 1)
                ins.then_inc(start_used, 1)

            def turn_mods():
                pe.wait_ge(start_rows_ready, 2)
                for bank, blocks in ((1, [0]), (0, range(1, KB))):
                    for i in [k + b for k in (0, KB) for b in blocks]:
                        ins = nc.tensor.matmul(aux(bank)[:, 2 * i:2 * i + 2], start_rows[0:2, i * P:i * P + P],
                                               ident[0:2, 0:2], start=True, stop=True)
                    ins.then_inc(start_turned, 1)

            def slabs(first, n, *rest):
                uses = pair_uses(first)
                with pe.Fori(0, n) as i:
                    for p in range(2):
                        slab(p, 2 * i + (first + p), i + uses, *rest)

            def sum_squares(name, ncol):
                s = norms[name]
                for part, (buf, wait) in enumerate(((sq_sum, (s["sq_added"], KB - 2)), (sq[1], (s["sq_ready"], KB)))):
                    pe.wait_ge(*wait)
                    for c in range(ncol // P):
                        ins = nc.tensor.matmul(aux(2)[:, c:c + 1], buf[:, c * P:c * P + P], ones[:, 0:1],
                                               start=part == 0 and c == 0, stop=True, skip_group_check=True)
                ins.then_inc(s["sums_done"], 1)

            def slabs_into_norm(first, order, hi, lo, cols, ready, name, free):
                ncol = cols[-1][1]
                rest = (order, hi, lo, cols, ready)
                first_pair(first, *rest, last_late(len(order), 2 if ncol > T else 4))
                slabs(first + 2, KB // 2 - 1, *rest)
                for w in free:
                    pe.wait_ge(*w)
                sum_squares(name, ncol)
                spread_roots(name, ncol)

            def spread_roots(name, ncol):
                s = norms[name]
                pe.wait_ge(s["rinv_ready"], 1)
                for c in range(ncol // P):
                    ins = nc.tensor.matmul(aux23[:, c * P:c * P + P], rinv[:, c:c + 1].to_broadcast([P, P]),
                                           ident[:, :], start=True, stop=True)
                    if c in (NLC - 1, NLC + NCC - 1):
                        ins.then_inc(s["rbc_ready"], 1)

            pe.wait_ge(fills, 2)
            all_k = list(range(KB))
            for l in range(DEPTH):
                s = S[l]
                both, lat = [(0, T), (T, TC)], [(0, T)]
                cols = both if l == 0 else lat
                n1, n2 = norms[f"n1_{l}"], norms[f"n2_{l}"]
                if l == 0:
                    pe.wait_ge(c_ready, 1)
                    for k in range(KB):
                        start_mods(k)
                        if k == KB - 2:
                            pe.wait_ge(first_loaded, 16 * 3)
                            sum_squares("n1_0", TC)
                    spread_roots("n1_0", TC)
                    turn_mods()

                def parts_ready(hi_sem, lo_sem, per):
                    return lambda n: ((hi_sem, per * (n + 1)), (lo_sem, per * (n + 1)))

                first_pair(PLAN[l, "kv"], all_k, h_hi, h_lo, both, parts_ready(n1["hi_ready"], n1["h_ready"], 2),
                           in_turns(KB, 3))
                slabs(PLAN[l, "kv"] + 2, HB - 1, all_k, h_hi, h_lo, both, None)
                n = 0
                for j in range(HB):
                    q = PLAN[l, "q"] + j
                    if j == 1:
                        pe.wait_ge(*drained_by(PLAN[l, "kv"] + 2 * HB - 1))
                        pe.wait_ge(n1["nt_ready"], 2 * KB)
                    elif j == 3:
                        pe.wait_ge(s["roped"], HB)
                    begin(j % 2, q, pair_uses(q - j % 2))
                    for k in range(KB):
                        tile(j % 2, k, all_k, h_hi, h_lo, cols, None)
                        if j % 2 == 0 or k >= NLC + NCC:
                            continue
                        if n >= 2:
                            last = n - 2
                            if last < NLC + NCC:
                                pe.wait_ge(s["v_moved"], last + 1)
                            else:
                                pe.wait_ge(s["k_moved"], last - (NLC + NCC) + 1)
                        src = Y if j == 1 else kT
                        for b in range(HB):
                            ins = nc.tensor.transpose(aux(2 + n % 2)[:, b * P:b * P + P], src[:, b, k * CH:k * CH + CH],
                                                      ident[:, :])
                        ins.then_inc(s["tr_done"], 1)
                        n += 1

                pe.wait_ge(s["k_moved"], NLC + NCC)
                n_state = n_chunk = 0

                def misc_free():
                    if n_state:
                        pe.wait_ge(s["state_ready"], 2 * n_state)
                    if n_chunk:
                        pe.wait_ge(s["o_ready"], n_chunk)

                for item in mixer_plan(l):
                    if item[0] == "tile":
                        _, phase, j, k = item
                        slab_ = PLAN[l, phase] + j
                        if k == 0:
                            begin(j % 2, slab_, pair_uses(slab_ - j % 2))
                        tile(j % 2, k, all_k, h_hi, h_lo, cols, None)
                        continue
                    if item[0] == "state":
                        _, d, c, prev, nxt = item
                        misc_free()
                        n_state += 1
                        pe.wait_ge(s["vz_ready"], n_state)
                        for b in range(HB):
                            ins = nc.tensor.matmul(aux(3)[:, b * P:b * P + P], ktok[:, c, b * P:b * P + P],
                                                   vz[:, 2 * b:2 * b + 2, :], start=True, stop=True)
                        ins.then_inc(s["u_done"], 1)
                        continue
                    name, c, col, fwd, bwd = item
                    if name == "scores":
                        if n_chunk == 0:
                            pe.wait_ge(s["roped"], 2 * HB)
                            if l == 0:
                                pe.wait_ge(mod_used, sum(MODS_KVQ))
                        else:
                            pe.wait_ge(s["St_ready"], 2 * n_chunk)
                        for hh in range(2):
                            r = slice(HD * hh, HD * hh + HD)
                            for b in range(HB):
                                ins = nc.tensor.matmul(aux(hh)[:, b * CH:b * CH + CH], kT[r, b, col:col + CH],
                                                       Y[r, b, col:col + CH], start=True, stop=True)
                        ins.then_inc(s["scores_done"], 1)
                    elif name == "out":
                        pe.wait_ge(s["qxi_ready"], 2 * (n_chunk + 1))
                        pe.wait_ge(s["state_ready"], 2 * n_state)
                        pe.wait_ge(s["St_ready"], 2 * (n_chunk + 1))
                        if n_chunk:
                            pe.wait_ge(s["osq_ready"], n_chunk)
                        for b in range(HB):
                            out = aux(2)[:, b * CH:b * CH + CH]
                            begun = False
                            for d, st in ((0, fwd), (1, bwd)):
                                if st is not None:
                                    nc.tensor.matmul(out, state[st[0]][:, st[1], b, :], qxi[:, d, b, :],
                                                     start=not begun, stop=True, skip_group_check=begun)
                                    begun = True
                            for hh in range(2):
                                r = slice(HD * hh, HD * hh + HD)
                                ins = nc.tensor.matmul(aux(2)[r, b * CH:b * CH + CH],
                                                       vtok[:, c, (2 * b + hh) * HD:(2 * b + hh + 1) * HD],
                                                       St[:, hh, b, :], start=False, stop=True, skip_group_check=True)
                        ins.then_inc(s["o_done"], 1)
                    elif name == "sums":
                        misc_free()
                        pe.wait_ge(s["osq_ready"], n_chunk + 1)
                        for b in range(HB):
                            ins = nc.tensor.matmul(aux(3)[:, 2 * b:2 * b + 2], osq[:, b, :], small[:, 0:2],
                                                   start=True, stop=True)
                        ins.then_inc(s["hsum_done"], 1)
                    else:
                        pe.wait_ge(s["hrinv_ready"], n_chunk + 1)
                        for b in range(HB):
                            for hh in range(2):
                                ins = nc.tensor.matmul(aux(3)[HD * hh:HD * hh + HD, b * CH:b * CH + CH],
                                                       rinv[:, 2 * b + hh:2 * b + hh + 1].to_broadcast([P, HD]),
                                                       ident[:, :], start=True, stop=True)
                        ins.then_inc(s["hbc_done"], 1)
                        n_chunk += 1

                pe.wait_ge(consts_loaded, 16 * 4)

                def channels(n):
                    if n >= 2:
                        pe.wait_ge(s["G_split"], n - 1)
                    col = n * CH
                    for b in range(FB):
                        ins = nc.tensor.matmul(aux(n % 2)[:, b * 2 * P:(b + 1) * 2 * P], Y[:, 4 + b, col:col + CH],
                                               chan[:, :], start=True, stop=True)
                    ins.then_inc(s["G_done"], 1)

                pe.wait_ge(s["St_ready"], 2 * n_chunk)
                pe.wait_ge(s["o_ready"], n_chunk)
                nd = dft_slabs(l)
                channels(0)
                for n in range(nd):
                    if n + 1 < nd:
                        channels(n + 1)
                    sl, p = PLAN[l, "dft"] + n, n % 2
                    w = T if n < NLC else C
                    pe.wait_ge(split, 2 * sl + 2)
                    pe.wait_ge(s["G_split"], n + 1)
                    first, last = n in (0, NLC), n in (NLC - 1, nd - 1)
                    for b in range(FB):
                        for t in range(2):
                            g = slice((2 * b + t) * P, (2 * b + t + 1) * P)
                            for k, (G, W) in enumerate(((G_hi, w_hi), (G_lo, w_hi), (G_hi, w_lo))):
                                if n < NLC:
                                    ins = nc.tensor.matmul(aux(2 + b)[:, 0:w], G[:, n % NLC, g],
                                                           W[p][:, t * w:(t + 1) * w], start=first and t == 0 and k == 0,
                                                           stop=last and t == 1 and k == 2)
                                else:
                                    ins = nc.tensor.matmul(aux(0)[:, b * w:(b + 1) * w], G[:, n % NLC, g],
                                                           W[p][:, t * w:(t + 1) * w],
                                                           start=first and b == 0 and t == 0 and k == 0, stop=True,
                                                           skip_group_check=True)
                    ins.then_inc(done, 1)
                slabs_into_norm(PLAN[l, "out"], Y_ORDER, h_hi, h_lo, cols, parts_ready(s["y_hi"], s["y_split"], 1),
                                f"n2_{l}", [(s["four_ready"], FB * len(cols))])
                u = 0
                for g, n in enumerate(GROUPS):
                    up, down = PLAN[l, "up", g], PLAN[l, "down", g]
                    if g == 0:
                        first_pair(up, all_k, h_hi, h_lo, cols, parts_ready(n2["hi_ready"], n2["h_ready"], len(cols)),
                                   in_turns(KB, 3))
                    slabs(up + 2 * (g == 0), n - (g == 0), all_k, h_hi, h_lo, cols, None)
                    rest = (list(range(n)), hid_hi, hid_lo, cols,
                            lambda k: ((s["hid_hi_ready"], u + k + 1), (s["hid_ready"], u + k + 1)))
                    if g < len(GROUPS) - 1:
                        first_pair(down, *rest, last_late(n, 2 if l == 0 else 4))
                        slabs(down + 2, KB // 2 - 1, *rest)
                    else:
                        slabs_into_norm(down, *rest, "final" if l else "n1_1", [(n2["nt_ready"], KB * len(cols))])
                    u += n


def tables():
    i = np.arange(CH)
    diff = i[None, :] - i[:, None]
    parts = []
    rows = T // GRID_W
    n_freq = HD // 4
    freq = ROPE_BASE ** (-np.arange(n_freq, dtype=np.float64) / n_freq)
    row, colm = np.repeat(np.arange(rows), GRID_W), np.tile(np.arange(GRID_W), rows)
    ang = np.concatenate([row[:, None] * freq, colm[:, None] * freq], axis=-1).T
    parts.append(np.tile(np.cos(ang), (4, 1)))
    parts.append(np.tile(np.concatenate([-np.sin(ang), np.sin(ang)]), (2, 1)))
    scale = HD ** -0.5
    parts += [np.maximum(diff, 0), (diff >= 0) * scale, np.maximum(-diff, 0), (diff <= 0) * scale]
    parts += [np.tile(i + 1, (P, 1)), np.tile(CH - i, (P, 1))]
    parts.append(np.eye(P))
    c = np.arange(FG)
    phi = 2 * np.pi * np.outer(c, c) / FG
    for f in (np.cos, np.sin):
        parts.append(np.kron(np.eye(2), f(phi)) / np.sqrt(FG))
    parts.append(np.stack([np.arange(P) < HD, np.arange(P) >= HD, CH - 1 - np.arange(P), np.arange(P)], axis=1))
    return np.concatenate(parts, axis=1).astype(np.float32)


def token_tables(n):
    t = np.arange(n)
    th = 2 * np.pi * (np.outer(t, t) % n) / n
    both = np.concatenate([np.cos(th), -np.sin(th)], axis=1) / np.sqrt(n)
    out = np.zeros((n // P, P, 8 * P), np.float32)
    out[:, :, :2 * n] = both.reshape(n // P, P, 2 * n)
    return out


def tiles(w, row_blocks):
    cols = w.shape[1] // P
    a = w.reshape(row_blocks, P, cols, P).transpose(2, 1, 0, 3).reshape(cols, P, row_blocks * P)
    if row_blocks < 8:
        a = np.concatenate([a, np.zeros((cols, P, (8 - row_blocks) * P), a.dtype)], axis=2)
    return a


def kernel(x, c, ctx, c_ctx, w_mod, b_mod, w_in, ret_decay_logit, mix_conv_w, w_out, ffn_w_up, ffn_conv_w,
           ffn_w_down, final_norm_g):
    import concourse.bacc as bacc
    from concourse.bass_utils import run_bass_kernel_spmd

    slabs = []
    for l in range(DEPTH):
        w = tiles(np.asarray(w_in)[l], KB)
        k0, v0, g0, f0, cb0, cc0, ch0 = 4, 8, 12, 16, 18, 20, 22
        order = [b + j for j in range(HB) for b in (k0, v0)] + list(range(HB))
        order += [b + j for j in range(FB) for b in (cc0, ch0)] + [b + j for j in range(FB) for b in (cb0, f0)]
        slabs.append(w[order + list(range(g0, g0 + HB))])
        slabs.append(token_tables(T))
        if l == 0:
            slabs.append(token_tables(C))
        slabs.append(tiles(np.asarray(w_out)[l], KB))
        up = tiles(np.asarray(ffn_w_up)[l], KB)
        b = 0
        for n in GROUPS:
            slabs.append(up[[k for j in range(b, b + n) for k in (j, NHB + j)]])
            slabs.append(tiles(np.asarray(ffn_w_down)[l][b * P:(b + n) * P], n))
            b += n
    slabs = np.concatenate(slabs)
    wm = np.asarray(w_mod)
    start = np.concatenate([wm[0][:, k * D:(k + 1) * D] for k in (SC1, SH1)], axis=1).reshape(KB, P, 2 * D)
    mods = np.stack([wm[l, :, (k * KB + b) * P:(k * KB + b + 1) * P].T for l, k, b in MOD_ORDER[MOD_START:]])
    bm = np.asarray(b_mod)
    bmod = np.stack([bm[l, (k * KB + b) * P:(k * KB + b + 1) * P] for l, k, b in MOD_ORDER], axis=1)
    ffnw = np.asarray(ffn_conv_w).reshape(DEPTH, 3, 2 * NHB, P).transpose(3, 0, 2, 1).reshape(P, -1)
    mixw = np.asarray(mix_conv_w).reshape(DEPTH, 3, FB, P).transpose(3, 0, 2, 1).reshape(P, -1)
    fng = np.asarray(final_norm_g).reshape(KB, P).T
    lg = np.asarray(ret_decay_logit)
    logit = []
    for l in range(DEPTH):
        logit.append(np.broadcast_to(lg[l].reshape(1, 2 * H), (P, 2 * H)))
        logit.append(np.repeat(lg[l].reshape(2 * HB, 2).T, HD, axis=0))
    vecs = np.concatenate([bmod, ffnw, mixw, fng] + logit, axis=1)
    xs = np.concatenate([np.asarray(x)[0], np.asarray(ctx)[0]])
    arrays = {
        "x": xs.T.reshape(KB, P, TC).transpose(1, 0, 2), "c": np.asarray(c).reshape(1, D),
        "c_ctx": np.asarray(c_ctx).reshape(1, D),
        "c_cols": np.stack([np.asarray(c).reshape(KB, P).T, np.asarray(c_ctx).reshape(KB, P).T], axis=2),
        "slabs": slabs, "start_mods": start, "mods": mods, "vecs": vecs, "tables": tables(),
    }
    arrays = {f"in_{k}": np.ascontiguousarray(v) for k, v in arrays.items()}
    nc = bacc.Bacc("TRN2", target_bir_lowering=False, num_devices=1)
    io = {k[3:]: nc.dram_tensor(k, v.shape, mybir.dt.from_np(v.dtype), kind="ExternalInput").ap()
          for k, v in arrays.items()}
    io["out"] = nc.dram_tensor("out", (KB, P, T), mybir.dt.float32, kind="ExternalOutput").ap()
    build_program(nc, io)
    r = run_bass_kernel_spmd(nc, [arrays], core_ids=[0])
    out = r.results[0]["out"]
    return np.ascontiguousarray(out.reshape(D, T).T).reshape(1, T, D)
```
